# Optimizing a Trainium2 kernel written in Bass

```python
import jax, jax.numpy as jnp
from jax import lax
import numpy as np
import math

D_MODEL = 1024
BATCH = 1
SEQ = 512
DEPTH = 1

GRID_W = 64
CTX_LEN = 256
N_MIXERS = 2
N_A_LAYERS = (DEPTH + N_MIXERS - 1) // N_MIXERS
N_B_LAYERS = DEPTH // N_MIXERS
POOL_WINDOWS = (2, 4, 8, 16)
POOL_GROUPS = 4
POOL_GROUP_DIM = D_MODEL // POOL_GROUPS
NA_HEADS = 16
NA_HEAD_DIM = D_MODEL // NA_HEADS
WIN_H = 8
WIN_W = 16
COL_BAND = 2 * WIN_W
D_FF = 2816
CONV_W = 3
ADA_CHUNKS = 6
EPS = 1e-6
NEG_INF = -1e30


def rms_norm(x, g):
    x32 = x.astype(jnp.float32)
    y = x32 * lax.rsqrt(jnp.mean(x32 * x32, axis=-1, keepdims=True) + EPS)
    return (y * g.astype(jnp.float32)).astype(x.dtype)

def modulate(h, shift, scale):
    return h * (1 + scale) + shift

def ada_mods(cond, w, b):
    mods = (jax.nn.silu(cond) @ w + b)[..., None, :]
    return jnp.split(mods, ADA_CHUNKS, axis=-1)

def centred_window_mean(u, w):
    n = u.shape[1]
    u32 = u.astype(jnp.float32)
    cs = jnp.concatenate([jnp.zeros_like(u32[:, :1]), jnp.cumsum(u32, axis=1)], axis=1)
    t = jnp.arange(n)
    lo = jnp.maximum(t - w // 2, 0)
    hi = jnp.minimum(t + w // 2, n)
    cnt = (hi - lo).astype(jnp.float32)
    return ((cs[:, hi] - cs[:, lo]) / cnt[None, :, None]).astype(u.dtype)

def pool_mixer(u, w_groups, scale):
    outs = []
    for g, win in enumerate(POOL_WINDOWS):
        ug = u[..., g * POOL_GROUP_DIM:(g + 1) * POOL_GROUP_DIM]
        outs.append((centred_window_mean(ug, win) - ug) @ w_groups[g])
    return jnp.concatenate(outs, axis=-1) * scale

def depthwise_conv(h, w, b):
    n = h.shape[1]
    p = CONV_W // 2
    hp = jnp.pad(h, ((0, 0), (p, p), (0, 0)))
    out = b
    for j in range(CONV_W):
        out = out + hp[:, j:j + n] * w[j]
    return out

def conv_ffn(u, w_up, conv_w, conv_b, w_down):
    h = depthwise_conv(u @ w_up, conv_w, conv_b)
    gate, val = jnp.split(h, 2, axis=-1)
    return (jax.nn.gelu(gate) * val) @ w_down

def column_band_tables():
    n_cb = GRID_W // WIN_W
    qcol = np.arange(GRID_W).reshape(n_cb, WIN_W)
    band_start = np.clip(np.arange(n_cb) * WIN_W - WIN_W // 2, 0, GRID_W - COL_BAND)
    band = band_start[:, None] + np.arange(COL_BAND)[None]
    win_start = np.clip(qcol - WIN_W // 2, 0, GRID_W - WIN_W)
    kc = band[:, None, :]
    valid = (kc >= win_start[..., None]) & (kc < win_start[..., None] + WIN_W)
    dc = np.clip(kc - qcol[..., None] + WIN_W - 1, 0, 2 * WIN_W - 2)
    return band, valid, dc

def split_heads(t, n_parts):
    bsz, n, _ = t.shape
    t = t.reshape(bsz, n, n_parts, NA_HEADS, NA_HEAD_DIM)
    return [jnp.transpose(t[:, :, j], (0, 2, 1, 3)) for j in range(n_parts)]

def context_self_attention(uc, w_qkv, w_o):
    bsz, m, _ = uc.shape
    q_c, k_c, v_c = split_heads(uc @ w_qkv, 3)
    s = jnp.einsum('bhqd,bhkd->bhqk', q_c, k_c).astype(jnp.float32) * (NA_HEAD_DIM ** -0.5)
    p = jax.nn.softmax(s, axis=-1).astype(v_c.dtype)
    o = jnp.einsum('bhqk,bhkd->bhqd', p, v_c)
    return jnp.transpose(o, (0, 2, 1, 3)).reshape(bsz, m, D_MODEL) @ w_o

def neighbourhood_attention(u, uc, w_qkv, w_o, rpb):
    bsz, n, _ = u.shape
    rows = n // GRID_W
    kh = min(WIN_H, rows)
    n_cb = GRID_W // WIN_W
    nk = kh * COL_BAND
    scale = NA_HEAD_DIM ** -0.5
    band, valid, dc = column_band_tables()
    band_idx = jnp.asarray(band)
    col_valid = jnp.asarray(valid)
    dc_idx = jnp.asarray(dc)

    q, k, v = [t.reshape(bsz, NA_HEADS, rows, GRID_W, NA_HEAD_DIM) for t in split_heads(u @ w_qkv, 3)]
    k_c, v_c = split_heads(uc @ w_qkv[:, D_MODEL:], 2)

    def row_block(r):
        s0 = jnp.clip(r - kh // 2, 0, rows - kh)
        q_r = lax.dynamic_index_in_dim(q, r, axis=2, keepdims=False)
        q_r = q_r.reshape(bsz, NA_HEADS, n_cb, WIN_W, NA_HEAD_DIM)

        def gather_band(t):
            t_r = lax.dynamic_slice_in_dim(t, s0, kh, axis=2)
            t_b = t_r[:, :, :, band_idx]
            return jnp.moveaxis(t_b, 3, 2).reshape(bsz, NA_HEADS, n_cb, nk, NA_HEAD_DIM)

        k_b, v_b = gather_band(k), gather_band(v)
        dr_idx = s0 + jnp.arange(kh) - r + WIN_H - 1
        bias = rpb[:, dr_idx[:, None, None, None], dc_idx[None]]
        bias = jnp.where(col_valid[None, None], bias.astype(jnp.float32), NEG_INF)
        bias = jnp.moveaxis(bias, 1, 3).reshape(NA_HEADS, n_cb, WIN_W, nk)
        s_lat = jnp.einsum('bhnqd,bhnkd->bhnqk', q_r, k_b).astype(jnp.float32) * scale + bias
        s_ctx = jnp.einsum('bhnqd,bhcd->bhnqc', q_r, k_c).astype(jnp.float32) * scale
        p = jax.nn.softmax(jnp.concatenate([s_lat, s_ctx], axis=-1), axis=-1).astype(v.dtype)
        o = (jnp.einsum('bhnqk,bhnkd->bhnqd', p[..., :nk], v_b)
             + jnp.einsum('bhnqc,bhcd->bhnqd', p[..., nk:], v_c))
        return o.reshape(bsz, NA_HEADS, GRID_W, NA_HEAD_DIM)

    o = lax.map(row_block, jnp.arange(rows))
    return jnp.transpose(o, (1, 0, 3, 2, 4)).reshape(bsz, n, D_MODEL) @ w_o

def first_inputs(seed: int = 0) -> dict:
    key = jax.random.key(seed)
    ks = jax.random.split(key, 19)
    D = D_MODEL
    G = POOL_GROUP_DIM

    def nrm(k, shape, s):
        return jax.random.normal(k, shape, jnp.float32) * s

    return {
        'x': nrm(ks[0], (BATCH, SEQ, D), 1.0),
        'c': nrm(ks[1], (BATCH, D), 1.0),
        'ctx': nrm(ks[2], (BATCH, CTX_LEN, D), 1.0),
        'c_ctx': nrm(ks[3], (D,), 1.0),
        'ada_w': nrm(ks[4], (DEPTH, D, ADA_CHUNKS * D), 0.5 * D ** -0.5),
        'ada_b': nrm(ks[5], (DEPTH, ADA_CHUNKS * D), 0.02),
        'mix_pre_g': 1.0 + nrm(ks[6], (DEPTH, D), 0.05),
        'mix_post_g': 1.0 + nrm(ks[7], (DEPTH, D), 0.05),
        'ffn_pre_g': 1.0 + nrm(ks[8], (DEPTH, D), 0.05),
        'ffn_post_g': 1.0 + nrm(ks[9], (DEPTH, D), 0.05),
        'pool_w': nrm(ks[10], (N_A_LAYERS, POOL_GROUPS, G, G), G ** -0.5),
        'pool_scale': 1.0 + nrm(ks[11], (N_A_LAYERS, D), 0.1),
        'na_w_qkv': nrm(ks[12], (N_B_LAYERS, D, 3 * D), D ** -0.5),
        'na_w_o': nrm(ks[13], (N_B_LAYERS, D, D), D ** -0.5),
        'na_rpb': nrm(ks[14], (N_B_LAYERS, NA_HEADS, 2 * WIN_H - 1, 2 * WIN_W - 1), 0.5),
        'ffn_w_up': nrm(ks[15], (DEPTH, D, 2 * D_FF), D ** -0.5),
        'ffn_conv_w': nrm(ks[16], (DEPTH, CONV_W, 2 * D_FF), CONV_W ** -0.5),
        'ffn_conv_b': nrm(ks[17], (DEPTH, 2 * D_FF), 0.02),
        'ffn_w_down': nrm(ks[18], (DEPTH, D_FF, D), D_FF ** -0.5),
    }

def first_block(x, c, ctx, c_ctx, ada_w, ada_b, mix_pre_g, mix_post_g, ffn_pre_g, ffn_post_g,
              pool_w, pool_scale, na_w_qkv, na_w_o, na_rpb,
              ffn_w_up, ffn_conv_w, ffn_conv_b, ffn_w_down):
    for i in range(DEPTH):
        last = i == DEPTH - 1
        j = i // N_MIXERS
        sh1, sc1, g1, sh2, sc2, g2 = ada_mods(c, ada_w[i], ada_b[i])
        csh1, csc1, cg1, csh2, csc2, cg2 = ada_mods(c_ctx, ada_w[i], ada_b[i])

        u = modulate(rms_norm(x, mix_pre_g[i]), sh1, sc1)
        if i % N_MIXERS == 0:
            y = pool_mixer(u, pool_w[j], pool_scale[j])
            if not last:
                uc = modulate(rms_norm(ctx, mix_pre_g[i]), csh1, csc1)
                yc = pool_mixer(uc, pool_w[j], pool_scale[j])
        else:
            uc = modulate(rms_norm(ctx, mix_pre_g[i]), csh1, csc1)
            y = neighbourhood_attention(u, uc, na_w_qkv[j], na_w_o[j], na_rpb[j])
            if not last:
                yc = context_self_attention(uc, na_w_qkv[j], na_w_o[j])
        x = x + g1 * rms_norm(y, mix_post_g[i])
        if not last:
            ctx = ctx + cg1 * rms_norm(yc, mix_post_g[i])

        f = conv_ffn(modulate(rms_norm(x, ffn_pre_g[i]), sh2, sc2),
                     ffn_w_up[i], ffn_conv_w[i], ffn_conv_b[i], ffn_w_down[i])
        x = x + g2 * rms_norm(f, ffn_post_g[i])
        if not last:
            fc = conv_ffn(modulate(rms_norm(ctx, ffn_pre_g[i]), csh2, csc2),
                          ffn_w_up[i], ffn_conv_w[i], ffn_conv_b[i], ffn_w_down[i])
            ctx = ctx + cg2 * rms_norm(fc, ffn_post_g[i])
    return x


DEPTH_2 = 2

N_GDN_LAYERS = (DEPTH_2 + N_MIXERS - 1) // N_MIXERS
N_GLA_LAYERS = DEPTH_2 // N_MIXERS
CHUNK = 64
CONV_K = 4

GDN_HEADS = 8
GDN_DK = 128
GDN_DV = 256
GDN_KEY = GDN_HEADS * GDN_DK
GDN_VAL = GDN_HEADS * GDN_DV
GDN_QKV = 2 * GDN_KEY + GDN_VAL
GDN_IN = GDN_QKV + GDN_VAL + 2 * GDN_HEADS

GLA_HEADS = 4
GLA_DK = 128
GLA_DV = 256
GLA_KEY = GLA_HEADS * GLA_DK
GLA_VAL = GLA_HEADS * GLA_DV
GLA_RANK = 16
GLA_GATE_NORM = 16.0
GLA_IN = 2 * GLA_KEY + 2 * GLA_VAL + GLA_RANK

DEEP_ALPHA = (2.0 * DEPTH_2) ** 0.25
DEEP_BETA = (8.0 * DEPTH_2) ** -0.25
LN_EPS = 1e-5
RMS_EPS = 1e-6
L2_EPS = 1e-6


def layer_norm(x, g, b):
    xf = x.astype(jnp.float32)
    mu = jnp.mean(xf, -1, keepdims=True)
    xc = xf - mu
    var = jnp.mean(xc * xc, -1, keepdims=True)
    y = xc * lax.rsqrt(var + LN_EPS) * g.astype(jnp.float32) + b.astype(jnp.float32)
    return y.astype(x.dtype)

def gated_rmsnorm(o, w, gate):
    o = o * lax.rsqrt(jnp.mean(o * o, -1, keepdims=True) + RMS_EPS)
    return o * w.astype(jnp.float32) * jax.nn.silu(gate.astype(jnp.float32))

def l2norm(t):
    return t * lax.rsqrt(jnp.sum(t * t, -1, keepdims=True) + L2_EPS)

def causal_conv_silu(x, w):
    y = lax.conv_general_dilated(
        x, w[:, None, :].astype(x.dtype), window_strides=(1,), padding=[(CONV_K - 1, 0)],
        dimension_numbers=('NWC', 'WIO', 'NWC'), feature_group_count=x.shape[-1])
    return jax.nn.silu(y)

def to_chunks(t):
    B, T, H, d = t.shape
    return t.reshape(B, T // CHUNK, CHUNK, H, d).transpose(0, 3, 1, 2, 4)

def from_scan_chunks(o):
    N, B, H, C, d = o.shape
    return o.transpose(1, 0, 3, 2, 4).reshape(B, N * C, H, d)

def gated_delta_rule(q, k, v, g, beta):
    B, T, H, dk = q.shape
    dv = v.shape[-1]
    q = to_chunks(q) * (dk ** -0.5)
    k = to_chunks(k)
    v = to_chunks(v)
    g = to_chunks(g[..., None])[..., 0]
    beta = to_chunks(beta[..., None])
    gc = jnp.cumsum(g, axis=-1)
    causal = jnp.tril(jnp.ones((CHUNK, CHUNK), bool))
    strict = jnp.tril(jnp.ones((CHUNK, CHUNK), bool), -1)
    diff = gc[..., :, None] - gc[..., None, :]
    decay = jnp.where(causal, jnp.exp(jnp.where(causal, diff, 0.0)), 0.0)
    kb = k * beta
    A = jnp.where(strict, jnp.einsum('bhncd,bhnsd->bhncs', kb, k) * decay, 0.0)
    eye = jnp.eye(CHUNK, dtype=A.dtype)
    rhs = jnp.concatenate([v * beta, kb * jnp.exp(gc)[..., None]], axis=-1)
    uw = lax.linalg.triangular_solve(A + eye, rhs, left_side=True, lower=True, unit_diagonal=True)
    u, w = uw[..., :dv], uw[..., dv:]
    qk = jnp.einsum('bhncd,bhnsd->bhncs', q, k) * decay
    q_dec = q * jnp.exp(gc)[..., None]
    k_dec = k * jnp.exp(gc[..., -1:] - gc)[..., None]
    g_last = jnp.exp(gc[..., -1])

    def step(S, inp):
        qk_n, qd_n, w_n, u_n, kd_n, gl_n = inp
        v_new = u_n - jnp.einsum('bhcd,bhde->bhce', w_n, S)
        o = jnp.einsum('bhcd,bhde->bhce', qd_n, S) + jnp.einsum('bhcs,bhse->bhce', qk_n, v_new)
        S = S * gl_n[..., None, None] + jnp.einsum('bhcd,bhce->bhde', kd_n, v_new)
        return S, o

    xs = tuple(jnp.moveaxis(a, 2, 0) for a in (qk, q_dec, w, u, k_dec, g_last))
    S0 = jnp.zeros((B, H, dk, dv), jnp.float32)
    _, o = lax.scan(step, S0, xs)
    return from_scan_chunks(o)

def gla_chunked(q, k, v, gk):
    B, T, H, dk = q.shape
    dv = v.shape[-1]
    q = to_chunks(q) * (dk ** -0.5)
    k = to_chunks(k)
    v = to_chunks(v)
    b = jnp.cumsum(to_chunks(gk), axis=3)
    causal = jnp.tril(jnp.ones((CHUNK, CHUNK), bool))[:, :, None]

    def step(S, inp):
        q_n, k_n, v_n, b_n = inp
        diff = b_n[:, :, :, None, :] - b_n[:, :, None, :, :]
        decay = jnp.exp(jnp.where(causal, diff, -jnp.inf))
        A = jnp.einsum('bhcsd,bhsd->bhcs', q_n[:, :, :, None, :] * decay, k_n)
        o = jnp.einsum('bhcd,bhde->bhce', q_n * jnp.exp(b_n), S) + jnp.einsum('bhcs,bhse->bhce', A, v_n)
        b_last = b_n[:, :, -1]
        S = S * jnp.exp(b_last)[..., None] + jnp.einsum(
            'bhcd,bhce->bhde', k_n * jnp.exp(b_last[:, :, None, :] - b_n), v_n)
        return S, o

    xs = tuple(jnp.moveaxis(a, 2, 0) for a in (q, k, v, b))
    S0 = jnp.zeros((B, H, dk, dv), jnp.float32)
    _, o = lax.scan(step, S0, xs)
    return from_scan_chunks(o)

def gdn_mixer(x, w_in, conv_w, a_log, dt_bias, norm_w, w_out):
    B, T, _ = x.shape
    f32 = jnp.float32
    p = x @ w_in
    qkv = causal_conv_silu(p[..., :GDN_QKV], conv_w)
    rest = p[..., GDN_QKV:]
    gate = rest[..., :GDN_VAL].reshape(B, T, GDN_HEADS, GDN_DV)
    b_logit = rest[..., GDN_VAL:GDN_VAL + GDN_HEADS].astype(f32)
    a_logit = rest[..., GDN_VAL + GDN_HEADS:].astype(f32)
    q = l2norm(qkv[..., :GDN_KEY].reshape(B, T, GDN_HEADS, GDN_DK).astype(f32))
    k = l2norm(qkv[..., GDN_KEY:2 * GDN_KEY].reshape(B, T, GDN_HEADS, GDN_DK).astype(f32))
    v = qkv[..., 2 * GDN_KEY:].reshape(B, T, GDN_HEADS, GDN_DV).astype(f32)
    beta = jax.nn.sigmoid(b_logit)
    g = -jnp.exp(a_log.astype(f32)) * jax.nn.softplus(a_logit + dt_bias.astype(f32))
    o = gated_delta_rule(q, k, v, g, beta)
    o = gated_rmsnorm(o, norm_w, gate)
    return o.reshape(B, T, GDN_VAL).astype(x.dtype) @ w_out

def gla_mixer(x, w_in, w_gk_up, b_gk, norm_w, w_out):
    B, T, _ = x.shape
    f32 = jnp.float32
    p = x @ w_in
    q = p[..., :GLA_KEY].reshape(B, T, GLA_HEADS, GLA_DK).astype(f32)
    k = p[..., GLA_KEY:2 * GLA_KEY].reshape(B, T, GLA_HEADS, GLA_DK).astype(f32)
    v = p[..., 2 * GLA_KEY:2 * GLA_KEY + GLA_VAL].reshape(B, T, GLA_HEADS, GLA_DV).astype(f32)
    gate = p[..., 2 * GLA_KEY + GLA_VAL:2 * GLA_KEY + 2 * GLA_VAL].reshape(B, T, GLA_HEADS, GLA_DV)
    gk_low = p[..., 2 * GLA_KEY + 2 * GLA_VAL:]
    gk_logit = (gk_low @ w_gk_up).astype(f32) + b_gk.astype(f32)
    gk = (jax.nn.log_sigmoid(gk_logit) / GLA_GATE_NORM).reshape(B, T, GLA_HEADS, GLA_DK)
    o = gla_chunked(q, k, v, gk)
    o = gated_rmsnorm(o, norm_w, gate)
    return o.reshape(B, T, GLA_VAL).astype(x.dtype) @ w_out

def second_inputs(seed: int = 0) -> dict:
    key = jax.random.key(seed)
    ks = jax.random.split(key, 16)
    f32 = jnp.float32

    def nrm(k, shape, s):
        return jax.random.normal(k, shape, f32) * s

    NA, NB, D = N_GDN_LAYERS, N_GLA_LAYERS, D_MODEL
    x = nrm(ks[0], (BATCH, SEQ, D), 1.0)
    gdn_col = jnp.concatenate([jnp.ones((2 * GDN_KEY,), f32), jnp.full((GDN_VAL,), DEEP_BETA, f32),
                               jnp.ones((GDN_VAL + 2 * GDN_HEADS,), f32)])
    gdn_w_in = nrm(ks[1], (NA, D, GDN_IN), D ** -0.5) * gdn_col
    gdn_conv_w = nrm(ks[2], (NA, CONV_K, GDN_QKV), CONV_K ** -0.5)
    gdn_a_log = jnp.log(jax.random.uniform(ks[3], (NA, GDN_HEADS), f32, 1.0, 16.0))
    dt = jnp.exp(jax.random.uniform(ks[4], (NA, GDN_HEADS), f32, math.log(1e-3), math.log(1e-1)))
    gdn_dt_bias = dt + jnp.log(-jnp.expm1(-dt))
    gdn_norm_w = 1.0 + nrm(ks[5], (NA, GDN_DV), 0.02)
    gdn_w_out = nrm(ks[6], (NA, GDN_VAL, D), (GDN_VAL ** -0.5) * DEEP_BETA)

    gla_col = jnp.concatenate([jnp.ones((2 * GLA_KEY,), f32), jnp.full((GLA_VAL,), DEEP_BETA, f32),
                               jnp.ones((GLA_VAL + GLA_RANK,), f32)])
    gla_w_in = nrm(ks[7], (NB, D, GLA_IN), D ** -0.5) * gla_col
    gla_w_gk_up = nrm(ks[8], (NB, GLA_RANK, GLA_KEY), GLA_RANK ** -0.5)
    gla_b_gk = nrm(ks[9], (NB, GLA_KEY), 0.1)
    gla_norm_w = 1.0 + nrm(ks[10], (NB, GLA_DV), 0.02)
    gla_w_out = nrm(ks[11], (NB, GLA_VAL, D), (GLA_VAL ** -0.5) * DEEP_BETA)

    ln_g = 1.0 + nrm(ks[12], (DEPTH_2, D), 0.02)
    ln_b = nrm(ks[13], (DEPTH_2, D), 0.02)
    return {"x": x, "gdn_w_in": gdn_w_in, "gdn_conv_w": gdn_conv_w, "gdn_a_log": gdn_a_log,
            "gdn_dt_bias": gdn_dt_bias, "gdn_norm_w": gdn_norm_w, "gdn_w_out": gdn_w_out,
            "gla_w_in": gla_w_in, "gla_w_gk_up": gla_w_gk_up, "gla_b_gk": gla_b_gk,
            "gla_norm_w": gla_norm_w, "gla_w_out": gla_w_out, "ln_g": ln_g, "ln_b": ln_b}

def second_block(x, gdn_w_in, gdn_conv_w, gdn_a_log, gdn_dt_bias, gdn_norm_w, gdn_w_out,
              gla_w_in, gla_w_gk_up, gla_b_gk, gla_norm_w, gla_w_out, ln_g, ln_b):
    for i in range(DEPTH_2):
        j = i // N_MIXERS
        if i % N_MIXERS == 0:
            y = gdn_mixer(x, gdn_w_in[j], gdn_conv_w[j], gdn_a_log[j], gdn_dt_bias[j],
                          gdn_norm_w[j], gdn_w_out[j])
        else:
            y = gla_mixer(x, gla_w_in[j], gla_w_gk_up[j], gla_b_gk[j], gla_norm_w[j], gla_w_out[j])
        x = layer_norm(DEEP_ALPHA * x + y, ln_g[i], ln_b[i])
    return x


def setup_inputs(seed=0):
    out = dict(first_inputs(seed))
    for name, value in second_inputs(seed + 1).items():
        if name != "x":
            out[name + "_2"] = value
    return out


def reference(
    x, c, ctx, c_ctx, ada_w, ada_b, mix_pre_g, mix_post_g, ffn_pre_g, ffn_post_g, pool_w,
    pool_scale, na_w_qkv, na_w_o, na_rpb, ffn_w_up, ffn_conv_w, ffn_conv_b, ffn_w_down,
    gdn_w_in_2, gdn_conv_w_2, gdn_a_log_2, gdn_dt_bias_2, gdn_norm_w_2, gdn_w_out_2, gla_w_in_2,
    gla_w_gk_up_2, gla_b_gk_2, gla_norm_w_2, gla_w_out_2, ln_g_2, ln_b_2,
):
    x = first_block(
        x, c, ctx, c_ctx, ada_w, ada_b, mix_pre_g, mix_post_g, ffn_pre_g, ffn_post_g, pool_w,
        pool_scale, na_w_qkv, na_w_o, na_rpb, ffn_w_up, ffn_conv_w, ffn_conv_b, ffn_w_down,
    )
    return second_block(
        x, gdn_w_in_2, gdn_conv_w_2, gdn_a_log_2, gdn_dt_bias_2, gdn_norm_w_2, gdn_w_out_2,
        gla_w_in_2, gla_w_gk_up_2, gla_b_gk_2, gla_norm_w_2, gla_w_out_2, ln_g_2, ln_b_2,
    )


_drawn_inputs = setup_inputs


def setup_inputs(seed=0):
    import zlib

    import numpy as np

    out = dict(_drawn_inputs(seed))
    spreads = {}
    factors = {'mix_pre_g': 3.259,
     'mix_post_g': 3.391,
     'ffn_pre_g': 2.707,
     'ffn_post_g': 3.387,
     'ffn_conv_b': 6.656,
     'gdn_norm_w_2': 8.0,
     'gla_b_gk_2': 6.773,
     'gla_norm_w_2': 8.0}
    for name, (base, spread) in spreads.items():
        noise = np.random.default_rng([zlib.crc32(name.encode()), seed]).standard_normal(out[name].shape)
        drawn = base * np.exp(spread * noise) if base else spread * noise
        out[name] = __import__('jax').numpy.asarray(drawn.astype(out[name].dtype))
    for name, factor in factors.items():
        out[name] = (out[name] * factor).astype(out[name].dtype)
    return out
```

```python
import concourse.bass as bass
from concourse import mybir
from concourse.alu_op_type import AluOpType as ALU
from contextlib import ExitStack

P = 128
T, D = 512, 1024
TT, KD = T // P, D // P
DFF = 2816
FC = DFF // P
POOL_GROUPS, POOL_WINDOWS = 4, (2, 4, 8, 16)
GDIM = D // POOL_GROUPS
BAND = P + 16
H, DK, DV = 8, 128, 256
LH = 4
UNIT = 2048
UC = UNIT // KD
LEVELS = 7
EPS, LN_EPS = 1e-6, 1e-5
ALPHA = 4.0 ** 0.25
GATE_NORM = 16.0
KEY_SCALE = DK ** -0.5

UP, DOWN = 2 * DFF // UC, DFF // (UNIT // D * P)
U_UP, U_DOWN = 0, UP
U_GIN = U_DOWN + DOWN
GIN_QK, GIN_V, GIN_GATE = 2 * H * DK // UC, H * DV // UC, H * DV // UC
U_GOUT = U_GIN + GIN_QK + GIN_V + GIN_GATE
GOUT = H * DV // (2 * P)
U_LIN = U_GOUT + GOUT
LIN_QK, LIN_V, LIN_GATE = 2 * LH * DK // UC, LH * DV // UC, LH * DV // UC
U_LOUT = U_LIN + LIN_QK + LIN_V + LIN_GATE
LOUT = LH * DV // (2 * P)
UNITS = U_LOUT + LOUT

NSCAL = 11
O_BANK = (6, 0, 2, 4)
GC, BSC, RK, RKI, KEG, KDS, VSC, GL, QA, QS, GLOG = range(NSCAL)


def band_start(tt):
    return max(P * tt - 8, 0)


def band_cols(tt):
    return min(P * tt + P + 8, T) - band_start(tt)


def build(nc, a, out, debug=None):
    f32, f32r, u32 = mybir.dt.float32, mybir.dt.float32r, mybir.dt.uint32
    ACT = mybir.ActivationFunctionType
    KB = 1024
    ds = bass.ds

    BASE = 16640
    CONST, RAW0 = BASE, BASE + 7680
    WH0 = RAW0 + 16 * KB
    WL0 = WH0 + 16 * KB
    XRES0 = WL0 + 16 * KB
    XTH0 = XRES0 + 16 * KB
    XTL0 = XTH0 + 16 * KB
    PH = XTL0 + 16 * KB

    def at(name, offset, shape, dt=f32):
        return nc.alloc_sbuf_tensor_at(name, [P, *shape], dt, offset=offset)

    ident = at("ident", CONST, [P])
    tri = at("tri", CONST + 512, [P])
    masks = at("masks", CONST + 1024, [LEVELS, P])
    conv_taps = at("conv_taps", CONST + 4608, [2, 2 * 2 * FC])
    scal_now = at("scal_now", CONST + 4608, [NSCAL, H])
    gdn_taps = at("gdn_taps", CONST + 5312, [4, 4 * KD])
    ones = at("ones", CONST + 5824, [8])
    c_col = at("c_col", CONST + 5856, [KD])
    bgk_col = at("bgk_col", CONST + 5888, [LH])
    scal = at("scal", CONST + 5920, [NSCAL, TT, H])
    stat = at("stat", CONST + 7328, [8, 8])
    glast_exp = at("glast_exp", CONST + 7584, [LH, TT])

    raw = at("raw", RAW0, [2, UNIT])
    wh = at("wh", WH0, [2, UNIT], f32r)
    wl = at("wl", WL0, [2, UNIT], f32r)

    xres = at("xres", XRES0, [TT, D])
    xth = at("xth", XTH0, [KD, T], f32r)
    xtl = at("xtl", XTL0, [KD, T], f32r)

    u_pool = at("u_pool", XTH0, [TT, D])
    y_pool = at("y_pool", XTH0, [TT, D])
    rows = at("rows", XTL0, [4, P])
    pooled = at("pooled", XTL0, [KD, T])
    mods = at("mods", PH, [6, D])
    gains = at("gains", PH + 24 * KB, [5, D])
    PRE1, POST1, PRE2, POST2, PSCALE = range(5)
    cond_bc = at("cond_bc", PH + 44 * KB, [KD, P])
    ada = at("ada", PH + 48 * KB, [4, KD, UC])
    pool_w = at("pool_w", PH + 80 * KB, [POOL_GROUPS, GDIM // P, GDIM])
    pool_band = at("pool_band", PH + 88 * KB, [POOL_GROUPS, TT, BAND])
    u_ffn = at("u_ffn", PH + 80 * KB, [TT, D])
    junk = at("junk", PH + 99 * KB, [D])

    conv_out = at("conv_out", PH, [2, 2, T])
    act_parts_h = at("act_parts_h", PH + 24 * KB, [4, T], f32r)
    act_parts_l = at("act_parts_l", PH + 32 * KB, [4, T], f32r)
    acts = at("acts", PH + 48 * KB, [FC, T])
    f_scaled = at("f_scaled", PH + 48 * KB, [TT, D])

    qkt = at("qkt", PH, [2, H, T])
    val = at("val", PH + 32 * KB, [TT, H, DV])
    gate = at("gate", PH + 64 * KB, [TT, H, DV])
    squares = at("squares", PH + 32 * KB, [2, 2, T])
    ba_raw = at("ba_raw", PH + 97 * KB, [KD, 2 * H])
    ba_h = at("ba_h", PH + 97 * KB + 512, [KD, 2 * H], f32r)
    ba_l = at("ba_l", PH + 97 * KB + 1024, [KD, 2 * H], f32r)
    ba_tmp = at("ba_tmp", PH + 97 * KB + 1536, [4, TT, H])
    norm_w = at("norm_w", PH + 96 * KB, [DV])
    alog_dt = at("alog_dt", PH + 99 * KB, [2, H])
    conv_v = at("conv_v", PH + 100 * KB, [2, T])
    state = at("state", PH + 96 * KB, [H, DV])
    D0 = XTH0
    tri_inv = at("tri_inv", D0, [H, P])
    k_now = at("k_now", D0, [H, P])
    tri_inv_t = at("tri_inv_t", D0 + 4 * KB, [H, P])
    k_dec = at("k_dec", D0 + 4 * KB, [H, P])
    upper = at("upper", D0 + 8 * KB, [H, P])
    k_in = at("k_in", D0 + 8 * KB, [H, P])
    upper_m = at("upper_m", D0 + 12 * KB, [H, P])
    gated_now = at("gated_now", D0 + 8 * KB, [H, DV])
    part = at("part", D0 + 16 * KB, [H, P])
    attn = at("attn", D0 + 20 * KB, [H, P])
    q_dec = at("q_dec", D0 + 24 * KB, [H, P])
    coef = at("coef", D0 + 28 * KB, [4, H])
    ogt_h = at("ogt_h", PH + 32 * KB, [TT, 2 * H, P], f32r)
    ogt_l = at("ogt_l", PH + 64 * KB, [TT, 2 * H, P], f32r)
    ln_gb = at("ln_gb", PH + 96 * KB, [2, D])
    bn = at("bn", PH + 16 * KB, [TT, 2, 6])
    mv = at("mv", PH + 17 * KB, [TT, 2])

    qg = at("qg", PH, [LH, T])
    kg = at("kg", PH + 8 * KB, [LH, T])
    bg = at("bg", PH + 16 * KB, [LH, T])
    vg = at("vg", PH + 24 * KB, [TT, LH, DV])
    gg = at("gg", PH + 40 * KB, [TT, LH, DV])
    eg = at("eg", PH + 56 * KB, [LH, T])
    zg = at("zg", PH + 64 * KB, [LH, T])
    attn_g = at("attn_g", PH + 72 * KB, [LH, T])
    kd_tok = at("kd_tok", PH + 80 * KB, [LH, TT, P])
    norm_w2 = at("norm_w2", PH + 88 * KB, [DV])
    low_raw = at("low_raw", PH + 89 * KB, [KD, 16])
    low_h = at("low_h", PH + 89 * KB + 512, [KD, 16], f32r)
    low_l = at("low_l", PH + 90 * KB, [KD, 16], f32r)
    gk_up = at("gk_up", PH + 91 * KB, [LH * DK])
    gk_low = at("gk_low", PH + 93 * KB, [T])
    junk_g = at("junk_g", PH + 95 * KB, [DV])
    states = at("states", PH, [TT - 1, LH, DV])
    bn2 = at("bn2", PH + 16 * KB, [TT, 2, 6])
    mv2 = at("mv2", PH + 17 * KB, [TT, 2])

    with ExitStack() as ctx:
        ps = ctx.enter_context(nc.psum_tensor("ps", [P, 8, 512], f32))
        made = {}

        def S(name):
            if name not in made:
                made[name] = ctx.enter_context(nc.semaphore(name))
            return made[name]

        raw_full = [S("raw_full0"), S("raw_full1")]
        hi_done = S("hi_done")
        unit_split = S("unit_split")
        w_used = S("w_used")
        ada_full = [S(f"ada_full{s}") for s in range(4)]

        def bank2(b):
            return ps[:, b:b + 2, :].rearrange("p b n -> p (b n)")

        def mm3(o, lh, ll, rh, rl, first, last):
            nc.tensor.matmul(o, lh, rh, start=first, stop=False)
            nc.tensor.matmul(o, lh, rl, start=False, stop=False)
            return nc.tensor.matmul(o, ll, rh, start=False, stop=last)

        block = ctx.enter_context(nc.Block())

        @block.sync
        def _(sp):
            def unit(u, src):
                slot, view = src
                sp.dma_start(raw[:, slot, :].rearrange("p (k n) -> p k n", k=view.shape[1]), view)\
                    .then_inc(raw_full[slot], 16)

            def cols(w, n):
                return w.rearrange("(k p) (u n) -> u p k n", p=P, n=n)

            def one(view, u):
                return view[ds(u, 1)].rearrange("a p k n -> p (a k) n")

            ada_v = cols(a["ada_w"][0], UC)
            w_up = a["ffn_w_up"][0].rearrange("(k p) (c u n) -> c u p k n", p=P, c=2, n=UC)
            w_down = a["ffn_w_down"][0].rearrange("(u k p) n -> u p k n", p=P, k=2)
            w_gin = cols(a["gdn_w_in_2"][0][:, 0:UC * (U_GOUT - U_GIN)], UC)
            w_gout = a["gdn_w_out_2"][0].rearrange("(u k p) n -> u p k n", p=P, k=2)
            w_lin = cols(a["gla_w_in_2"][0][:, 0:UC * (U_LOUT - U_LIN)], UC)
            w_lout = a["gla_w_out_2"][0].rearrange("(u k p) n -> u p k n", p=P, k=2)

            sp.dma_start(rows[0:KD, 0, :], a["c"][0].rearrange("(k n) -> k n", n=P)).then_inc(S("c_in"), 16)
            sp.dma_start(ident[:], a["consts"][:, 0:P]).then_inc(S("ident_in"), 16)
            for s in range(4):
                sp.dma_start(ada[:, s], ada_v[s]).then_inc(ada_full[s], 16)
            for tt in range(TT):
                sp.dma_start(xres[:, tt, :], a["x"][0, tt * P:(tt + 1) * P, :]).then_inc(S("x_in"), 16)
            with sp.Fori(1, 6) as i:
                for s in range(4):
                    sp.wait_ge(S("ada_used"), i * 4 + s - 3)
                    sp.dma_start(ada[:, s], one(ada_v, i * 4 + s)).then_inc(ada_full[s], 16)

            unit(0, (0, w_up[0, 0]))
            unit(1, (1, w_up[1, 0]))
            with sp.Fori(1, UP // 2) as i:
                for s in range(2):
                    sp.wait_ge(unit_split, i * 2 + s - 1)
                    unit(None, (s, one(w_up[s], i)))

            def stream(first, n, view):
                with sp.Fori(0, n // 2) as i:
                    for s in range(2):
                        sp.wait_ge(unit_split, first + i * 2 + s - 1)
                        unit(None, ((first + s) % 2, one(view, i * 2 + s)))
                if n % 2:
                    sp.wait_ge(unit_split, first + n - 2)
                    unit(None, ((first + n - 1) % 2, view[n - 1]))

            stream(U_DOWN, DOWN, w_down)
            stream(U_GIN, U_GOUT - U_GIN, w_gin)
            stream(U_GOUT, GOUT, w_gout)
            stream(U_LIN, U_LOUT - U_LIN, w_lin)
            stream(U_LOUT, LOUT, w_lout)

            for tt in range(TT):
                sp.wait_ge(S("ln2_done"), tt + 1)
                sp.dma_start(out[0, tt * P:(tt + 1) * P, :], xres[:, tt, :]).then_inc(S("out_written"), 16)
            sp.wait_ge(S("out_written"), 16 * TT)

        @block.gpsimd
        def _(pool):
            nc.gpsimd.memset(ones[:], 1.0).then_inc(S("ones_set"), 1)

            def low(u, s):
                pool.wait_ge(hi_done, u + 1)
                nc.gpsimd.tensor_tensor(wl[:, s, :], raw[:, s, :], wh[:, s, :].bitcast(f32), ALU.subtract)\
                    .then_inc(unit_split, 1)

            with pool.Fori(0, (U_GIN + 1) // 2) as i:
                for s in range(2):
                    low(i * 2 + s, s)
            first = (U_GIN + 1) // 2 * 2
            last = U_GOUT + 2
            with pool.Fori(0, (last - first) // 2) as i:
                for s in range(2):
                    low(first + i * 2 + s, s)
            if (last - first) % 2:
                low(last - 1, (last - 1) % 2)

            pool.wait_ge(S("gate_done"), GIN_GATE)
            pool.wait_ge(S("factors"), 8)
            nc.gpsimd.memset(state[:], 0.0).then_inc(S("state_zero"), 1)
            with pool.Fori(0, TT) as i:
                for g in range(2):
                    hs = slice(4 * g, 4 * g + 4)
                    pool.wait_ge(S("dec_exp"), i * 2 + g + 1)
                    nc.gpsimd.tensor_tensor(part[:, hs, :], part[:, hs, :],
                                            tri[:].unsqueeze(1).broadcast_to([P, 4, P]), ALU.mult)\
                        .then_inc(S("dec_done"), 1)
                for l in range(LEVELS):
                    for g in range(2):
                        hs = slice(4 * g, 4 * g + 4)
                        if l == 0:
                            pool.wait_ge(S("u_done"), i * 2 + g + 1)
                        elif l == 1:
                            pool.wait_ge(S("y0_done"), i * 2 + g + 1)
                        else:
                            pool.wait_ge(S("p1_mm"), i * 12 + 2 * (l - 2) + g + 1)
                        nc.gpsimd.tensor_tensor(upper_m[:, hs, :], upper[:, hs, :],
                                                masks[:, l, :].unsqueeze(1).broadcast_to([P, 4, P]), ALU.mult)\
                            .then_inc(S("um_done"), 1)

            with pool.Fori(0, (U_LIN + 1 - last) // 2) as i:
                for s in range(2):
                    low(last + i * 2 + s, (last + s) % 2)
            at_u = last + (U_LIN + 1 - last) // 2 * 2
            with pool.Fori(0, (UNITS - at_u) // 2) as i:
                for s in range(2):
                    low(at_u + i * 2 + s, (at_u + s) % 2)
            if (UNITS - at_u) % 2:
                low(UNITS - 1, (UNITS - 1) % 2)
        @block.scalar
        def _(act):
            def high(u, s, nth):
                act.wait_ge(raw_full[s], (nth + 1) * 16)
                if not (isinstance(u, int) and u < 2):
                    act.wait_ge(w_used, u - 1)
                nc.scalar.activation(wh[:, s, :], raw[:, s, :], ACT.Copy).then_inc(hi_done, 1)

            def high_at(first, i, s):
                high(first + s + i * 2, (first + s) % 2, i + (first + s) // 2)

            sums = [0]

            def square_sum(scratch, x, total):
                if sums[0]:
                    act.wait_ge(S("squares_summed"), sums[0])
                sums[0] += 1
                nc.scalar.activation(scratch, x, ACT.Square, accum_out=total).then_inc(S("squares_summed"), 1)

            roots = [0]

            def root(x):
                roots[0] += 1
                act.wait_ge(S("mean_done"), roots[0])
                nc.scalar.activation(x, x, ACT.Sqrt).then_inc(S("root_done"), 1)

            def parts_high(stage, tt, b):
                act.wait_ge(S("turned"), stage * TT + tt + 1)
                nc.scalar.activation(xth[:, :, tt * P:(tt + 1) * P],
                                     bank2(b).rearrange("p (k n) -> p k n", n=P), ACT.Copy).then_inc(S("parts_hi"), 1)

            def row(dst, src, name):
                act.dma_start(dst, src.partition_broadcast(P)).then_inc(S(name), 16)

            act.dma_start(rows[KD:KD + LH, 0, :], a["gla_b_gk_2"][0].rearrange("(k n) -> k n", n=P)).then_inc(S("rows_in"), 16)
            cw = a["ffn_conv_w"][0].rearrange("j (k n) -> (j k) n", n=P)
            cb = a["ffn_conv_b"][0].rearrange("(k n) -> k n", n=P)
            nch = 2 * FC
            act.dma_start(rows[0:2 * nch, 1, :], cw[0:2 * nch, :]).then_inc(S("rows_in"), 16)
            act.dma_start(rows[0:nch, 2, :], cw[2 * nch:3 * nch, :]).then_inc(S("rows_in"), 16)
            act.dma_start(rows[nch:2 * nch, 2, :], cb).then_inc(S("rows_in"), 16)
            act.dma_start(rows[:, 3, :], a["gdn_conv_w_2"][0].rearrange("j (k n) -> (j k) n", n=P)).then_inc(S("rows_in"), 16)
            act.dma_start(mods[:].rearrange("p j n -> p (j n)"),
                           a["ada_b"][0].partition_broadcast(P)).then_inc(S("ada_b_in"), 16)
            row(gains[:, PRE1, :], a["mix_pre_g"][0], "gains_in")
            act.dma_start(pool_band[:].rearrange("p g t n -> p (g t n)"), a["pool_band"]).then_inc(S("pool_in"), 16)
            act.dma_start(pool_w[:], a["pool_w"][0].rearrange("g (k p) n -> p g k n", p=P)).then_inc(S("pool_in"), 16)
            row(gains[:, PSCALE, :], a["pool_scale"][0], "gains_in")
            row(gains[:, POST1, :], a["mix_post_g"][0], "gains_in")
            row(gains[:, PRE2, :], a["ffn_pre_g"][0], "gains_in")
            row(gains[:, POST2, :], a["ffn_post_g"][0], "gains_in")
            act.dma_start(tri[:], a["consts"][:, P:2 * P]).then_inc(S("masks_in"), 16)
            act.dma_start(masks[:].rearrange("p l n -> p (l n)"), a["consts"][:, 2 * P:]).then_inc(S("masks_in"), 16)
            act.dma_start(ba_raw[:], a["gdn_w_in_2"][0][:, UC * (U_GOUT - U_GIN):].rearrange("(k p) n -> p k n", p=P))\
                .then_inc(S("ba_in"), 16)

            act.wait_ge(S("rows_turned"), 1)
            nc.scalar.activation(c_col[:], ps[:, 6, 0:KD], ACT.Silu).then_inc(S("c_silu"), 1)
            for tt in range(TT):
                act.wait_ge(S("x_in"), 16 * TT)
                square_sum(junk[:], xres[:, tt, :], stat[:, 0, tt:tt + 1])
            root(stat[:, 0, 0:TT])
            for cb in range(KD):
                act.wait_ge(S("pool_mm"), cb + 1)
                nc.scalar.activation(pooled[:, cb, :], ps[:, 4 + cb % 4, :], ACT.Copy).then_inc(S("pooled_done"), 1)
            high(0, 0, 0)
            high(1, 1, 0)
            for tt in range(TT):
                act.wait_ge(S("ys_done"), tt + 1)
                square_sum(junk[:], y_pool[:, tt, :], stat[:, 1, tt:tt + 1])
                root(stat[:, 1, tt:tt + 1])
                act.wait_ge(S("x1_done"), tt + 1)
                square_sum(junk[:], xres[:, tt, :], stat[:, 2, tt:tt + 1])
                root(stat[:, 2, tt:tt + 1])
            for tt in range(TT):
                parts_high(0, tt, 4 + 2 * (tt % 2))

            with act.Fori(0, UP // 2) as i:
                for s in range(2):
                    high_at(U_UP + 2, i, s)
                    for sub in range(2):
                        chunk = i * 2 + sub + s * FC
                        if sub == 0:
                            act.wait_ge(S("up_half"), i * 2 + s + 1)
                        else:
                            act.wait_ge(w_used, i * 2 + s + 1)
                        act.wait_ge(S("act_done"), i * 2 + sub + 1)
                        act.wait_ge(S("cols_done"), 3)
                        nc.scalar.activation(conv_out[:, s, sub, :], ps[:, 2 * s + sub, :], ACT.Identity,
                                             scale=conv_taps[:, 0, ds(chunk + 2 * FC, 1)],
                                             bias=conv_taps[:, 1, ds(chunk + 2 * FC, 1)]).then_inc(S("conv_mid"), 1)
                    if s == 0:
                        for sub in range(2):
                            act.wait_ge(S("conv_done"), i * 4 + sub + 5)
                            nc.scalar.activation(conv_out[:, 0, sub, :], conv_out[:, 0, sub, :], ACT.Gelu_apprx_tanh)\
                                .then_inc(S("gelu_done"), 1)
            with act.Fori(0, DOWN // 2) as i:
                for s in range(2):
                    high_at(U_DOWN + 2, i, s)
            high(U_DOWN + DOWN + 1, (U_DOWN + DOWN + 1) % 2, (U_DOWN + DOWN + 1) // 2)
            for tt in range(TT):
                act.wait_ge(S("proj_mm"), tt + 1)
                square_sum(junk[:], bank2(2 * tt), stat[:, 3, tt:tt + 1])
                root(stat[:, 3, tt:tt + 1])
            for tt in range(TT):
                parts_high(1, tt, 2 * tt)
            act.wait_ge(S("x2_done"), TT)
            row(norm_w[:], a["gdn_norm_w_2"][0], "alog_in")
            row(alog_dt[:, 0, :], a["gdn_a_log_2"][0], "alog_in")
            row(alog_dt[:, 1, :], a["gdn_dt_bias_2"][0], "alog_in")

            act.wait_ge(S("ba_ready"), 1)
            nc.scalar.activation(ba_tmp[:, 0], ba_tmp[:, 0], ACT.Exp, scale=-1.0).then_inc(S("ba_exp"), 1)
            nc.scalar.activation(ba_tmp[:, 2], ba_tmp[:, 2], ACT.Exp).then_inc(S("ba_exp"), 1)
            act.wait_ge(S("ba_exp"), 2)
            nc.scalar.activation(ba_tmp[:, 2], ba_tmp[:, 2], ACT.Ln, bias=1.0).then_inc(S("ba_exp"), 1)
            act.wait_ge(S("alog_in"), 48)
            nc.scalar.activation(alog_dt[:, 0, :], alog_dt[:, 0, :], ACT.Exp).then_inc(S("ba_exp"), 1)
            act.wait_ge(S("gc_ready"), 1)
            nc.scalar.activation(scal[:, KEG], scal[:, GC], ACT.Exp).then_inc(S("gc_exp"), 1)
            nc.scalar.activation(scal[:, KDS], scal[:, KDS], ACT.Exp).then_inc(S("gc_exp"), 1)
            nc.scalar.activation(scal[:, GL], ps[:, 7, 96:128].rearrange("p (t h) -> p t h", h=H), ACT.Exp).then_inc(S("gc_exp"), 1)

            def conv_first(i, s, base, free):
                for sub in range(2):
                    if sub == 0:
                        act.wait_ge(S("qkv_half"), base + i * 2 + s + 1)
                    else:
                        act.wait_ge(w_used, U_GIN + base + i * 2 + s + 1)
                    free(i, s, sub)
                    act.wait_ge(S("cols_done"), 3)
                    nc.scalar.activation(conv_v[:, sub, :], ps[:, 2 * s + sub, :], ACT.Copy,
                                         scale=gdn_taps[:, 3, ds(base * 2 + i * 4 + 2 * s + sub, 1)]).then_inc(S("tap3"), 1)

            qk_flat = qkt[:].rearrange("p a h t -> p (a h) t")
            act.sem_inc(S("qk_silu"), 2)

            def squashed(i, s, sub):
                act.wait_ge(S("qk_silu"), i * 4 + 2 * s + sub + 1)
            with act.Fori(0, GIN_QK // 2) as i:
                for s in range(2):
                    high_at(U_GIN + 2, i, s)
                    conv_first(i, s, 0, squashed)
                    for sub in range(2):
                        act.wait_ge(S("qkv_conv"), i * 4 + 2 * s + sub + 5)
                        act.wait_ge(S("parts_lo"), 2 * TT)
                        nc.scalar.activation(qk_flat[:, ds(i * 4 + 2 * s + sub, 1), :].rearrange("p a t -> p (a t)"),
                                             conv_v[:, sub, :], ACT.Silu).then_inc(S("qk_silu"), 1)
            act.wait_ge(S("qk_silu"), 2 + 2 * GIN_QK)
            with act.Fori(0, GIN_V // 2) as i:
                for s in range(2):
                    high_at(U_GIN + GIN_QK + 2, i, s)

                    def turned(i, s, sub):
                        act.wait_ge(S("v_turned"), i * 2 + s + 1)
                    conv_first(i, s, GIN_QK, turned)
                    for sub in range(2):
                        act.wait_ge(S("qkv_conv"), 2 * GIN_QK + i * 4 + 2 * s + sub + 5)
                        nc.scalar.activation(conv_v[:, sub, :], conv_v[:, sub, :], ACT.Silu).then_inc(S("v_silu"), 1)
            gate_flat = gate[:].rearrange("p t h v -> p t (h v)")
            with act.Fori(0, GIN_GATE // 2) as i:
                for s in range(2):
                    high_at(U_GIN + GIN_QK + GIN_V + 2, i, s)
                    act.wait_ge(w_used, U_GIN + GIN_QK + GIN_V + i * 2 + s + 1)
                    act.wait_ge(S("parts_lo"), 2 * TT)
                    nc.scalar.activation(gate_flat[:, :, ds((i * 2 + s) * UC, UC)],
                                         bank2(2 * s).rearrange("p (t n) -> p t n", n=UC), ACT.Silu).then_inc(S("gate_silu"), 1)
            root(scal[:, RKI].rearrange("p t h -> p (t h)"))
            root(scal[:, QS].rearrange("p t h -> p (t h)"))

            with act.Fori(0, TT) as i:
                for g in range(2):
                    hs = slice(4 * g, 4 * g + 4)
                    act.wait_ge(S("gcrow_mm"), i * 2 + g + 1)
                    nc.scalar.activation(upper_m[:, hs, :], ps[:, 4 + g, :].rearrange("p (h n) -> p h n", n=P), ACT.Exp)\
                        .then_inc(S("eg_done"), 1)
                    act.wait_ge(S("dec_diff"), i * 2 + g + 1)
                    nc.scalar.activation(part[:, hs, :], part[:, hs, :], ACT.Exp).then_inc(S("dec_exp"), 1)
                for g in range(2):
                    hs = slice(4 * g, 4 * g + 4)
                    act.wait_ge(S("x0_mm"), i * 2 + g + 1)
                    nc.scalar.activation(tri_inv_t[:, hs, :], ps[:, 2 * g, :].rearrange("p (h n) -> p h n", n=P), ACT.Copy)\
                        .then_inc(S("x0_done"), 1)
                for l in range(1, LEVELS):
                    for g in range(2):
                        hs = slice(4 * g, 4 * g + 4)
                        act.wait_ge(S("p1_mm"), i * 12 + 2 * (l - 1) + g + 1)
                        nc.scalar.activation(part[:, hs, :], ps[:, 2 * g, :].rearrange("p (h n) -> p h n", n=P), ACT.Copy)\
                            .then_inc(S("p1_done"), 1)
                for g in range(2):
                    act.wait_ge(S("um_done"), i * 14 + 13 + g)
                    act.wait_ge(S("ktok_mm"), i + 1)
                    for h in range(4 * g, 4 * g + 4):
                        ke = nc.scalar.activation(k_in[:, h, :], ps[:, 6 + g, (h % 4) * P:(h % 4 + 1) * P], ACT.Copy,
                                                  scale=scal_now[:, KEG, h:h + 1])
                    ke.then_inc(S("kin_done"), 1)
                for g in range(2):
                    hs = slice(4 * g, 4 * g + 4)
                    act.wait_ge(S("w_mm"), i * 2 + g + 1)
                    nc.scalar.activation(part[:, hs, :], ps[:, 2 * g, :].rearrange("p (h n) -> p h n", n=P), ACT.Copy, scale=-1.0)\
                        .then_inc(S("w_done"), 1)
                for h in range(H):
                    act.wait_ge(S("o_mm"), i * H + (h | 1) + 1)
                    sq = nc.scalar.activation(gated_now[:, h, :], ps[:, (0, 2, 6, 7)[h // 2], (h % 2) * DV:(h % 2 + 1) * DV], ACT.Square,
                                              accum_out=coef[:, 0, h:h + 1])
                sq.then_inc(S("o_ss"), 1)
                act.wait_ge(S("o_ms"), i + 1)
                nc.scalar.activation(coef[:, 1, :], coef[:, 1, :], ACT.Sqrt).then_inc(S("o_rt"), 1)
                for b in range(4):
                    act.wait_ge(S("og_turned"), i * 4 + b + 1)
                    act.wait_ge(S("gate_done"), GIN_GATE)
                    nc.scalar.activation(ogt_h[:, ds(i, 1), 4 * b:4 * b + 4, :].rearrange("p a k n -> p (a k) n"),
                                         ps[:, (1, 3, 4, 5)[b], :].rearrange("p (k n) -> p k n", n=P), ACT.Copy)\
                        .then_inc(S("ogt_hi"), 1)
            act.wait_ge(S("s_done"), TT * H)
            row(ln_gb[:, 0, :], a["ln_g_2"][0], "ln1_in")
            row(ln_gb[:, 1, :], a["ln_b_2"][0], "ln1_in")
            with act.Fori(0, GOUT // 2) as i:
                for s in range(2):
                    high_at(U_GOUT + 2, i, s)
            for tt in range(TT):
                root(mv[:, tt, 1:2])
            act.wait_ge(w_used, U_LIN)
            act.dma_start(low_raw[:], a["gla_w_in_2"][0][:, UC * (U_LOUT - U_LIN):].rearrange("(k p) n -> p k n", p=P))\
                .then_inc(S("low_in"), 16)
            act.dma_start(gk_up[0:16, :], a["gla_w_gk_up_2"][0]).then_inc(S("low_in"), 16)
            row(norm_w2[:], a["gla_norm_w_2"][0], "low_in")
            for tt in range(TT):
                parts_high(2, tt, 2 * tt)
            act.wait_ge(S("ln1_done"), TT)
            row(ln_gb[:, 0, :], a["ln_g_2"][1], "ln2_in")
            row(ln_gb[:, 1, :], a["ln_b_2"][1], "ln2_in")

            act.wait_ge(S("low_mm"), 1)
            nc.scalar.activation(gk_low[0:16, :], ps[0:16, 0, :], ACT.Copy).then_inc(S("gk_low_done"), 1)

            def qk_unit(j):
                u = U_LIN + j
                high(u + 2, u % 2, (u + 2) // 2)
                act.wait_ge(w_used, u + 1)
                dst = (qg if j < LIN_QK // 2 else kg)[:, 2 * (j % 2):2 * (j % 2) + 2, :]
                nc.scalar.activation(dst, ps[:, 2 * (j % 2):2 * (j % 2) + 2, :], ACT.Copy,
                                     scale=KEY_SCALE if j < LIN_QK // 2 else 1.0).then_inc(S("lqk_done"), 1)
            qk_unit(0)
            for h in range(LH):
                act.wait_ge(S("gk_mm"), h + 1)
                nc.scalar.activation(zg[:, h, :], ps[:, 4 + h, :], ACT.Identity, bias=bgk_col[:, h:h + 1]).then_inc(S("gk_z"), 1)
            act.wait_ge(S("gk_abs"), 1)
            nc.scalar.activation(eg[:], eg[:], ACT.Exp).then_inc(S("gk_exp"), 1)
            act.wait_ge(S("gk_exp"), 1)
            nc.scalar.activation(eg[:], eg[:], ACT.Ln, bias=1.0).then_inc(S("gk_exp"), 1)
            for j in range(1, LIN_QK):
                qk_unit(j)
            for j in range(LIN_V + LIN_GATE):
                u = U_LIN + LIN_QK + j
                if j >= 1:
                    act.wait_ge(S("lev_diff"), j)
                    nc.scalar.activation(eg[:], eg[:], ACT.Exp, scale=1.0 / GATE_NORM).then_inc(S("lev_exp"), 1)
                high(u + 2, u % 2, (u + 2) // 2)
                act.wait_ge(w_used, u + 1)
                src = bank2(2 * (j % 2)).rearrange("p (t n) -> p t n", n=UC)
                if j < LIN_V:
                    nc.scalar.activation(vg[:, :, j, :], src, ACT.Copy).then_inc(S("lv_done"), 1)
                else:
                    nc.scalar.activation(gg[:, :, j - LIN_V, :], src, ACT.Silu).then_inc(S("lv_done"), 1)
            act.wait_ge(S("lev_z"), LEVELS)
            nc.scalar.activation(eg[:], bg[:], ACT.Exp, scale=1.0 / GATE_NORM).then_inc(S("qe_exp"), 1)
            nc.scalar.activation(glast_exp[:], bg[:].rearrange("p h (t c) -> p h t c", c=P)[:, :, :, P - 1], ACT.Exp,
                                 scale=1.0 / GATE_NORM).then_inc(S("qe_exp"), 1)
            act.wait_ge(S("kd_diff"), 1)
            nc.scalar.activation(eg[:], eg[:], ACT.Exp, scale=1.0 / GATE_NORM).then_inc(S("kd_exp"), 1)
            for h in range(LH):
                act.wait_ge(S("kd_turned"), h + 1)
                nc.scalar.activation(kd_tok[:, h], ps[:, 4 + h, :].rearrange("p (t n) -> p t n", n=P), ACT.Copy).then_inc(S("kd_done"), 1)
            for tt in range(TT):
                for h in range(LH):
                    act.wait_ge(S("lo_mm"), tt * LH + (h | 1) + 1)
                    square_sum(junk_g[:], ps[:, O_BANK[tt] + h // 2, (h % 2) * DV:(h % 2 + 1) * DV], stat[:, 4 + tt, h:h + 1])
                root(stat[:, 4 + tt, 0:LH])
            for tt in range(TT):
                parts_high(3, tt, O_BANK[tt])
            for j in range(2, LOUT):
                high(U_LOUT + j, (U_LOUT + j) % 2, (U_LOUT + j) // 2)
            for tt in range(TT):
                root(mv2[:, tt, 1:2])
        @block.vector
        def _(v):
            V = nc.vector

            seen = {}

            def own(name):
                seen[name] = seen.get(name, 0) + 1
                v.wait_ge(S(name), seen[name])

            roots = [0]

            def inv_root(x, total, eps, count):
                v.wait_ge(S("squares_summed"), count)
                V.tensor_scalar(x, x, 1.0 / total, eps, ALU.mult, ALU.add).then_inc(S("mean_done"), 1)
                inverse(x)

            def inverse(x):
                roots[0] += 1
                v.wait_ge(S("root_done"), roots[0])
                V.reciprocal(x, x).then_inc(S("inverse_done"), 1)
                own("inverse_done")

            def parts_low(stage, tt, b):
                v.wait_ge(S("parts_hi"), stage * TT + tt + 1)
                cols = slice(tt * P, (tt + 1) * P)
                V.tensor_tensor(xtl[:, :, cols], bank2(b).rearrange("p (k n) -> p k n", n=P),
                                xth[:, :, cols].bitcast(f32), ALU.subtract).then_inc(S("parts_lo"), 1)

            v.wait_ge(S("rows_turned"), 1)
            v.wait_ge(S("c_silu"), 1)
            V.tensor_copy(bgk_col[:], ps[:, 6, KD:KD + LH]).then_inc(S("cols_done"), 1)
            V.tensor_copy(conv_taps[:].rearrange("p a n -> p (a n)"), ps[:, 7, 16:16 + 8 * FC]).then_inc(S("cols_done"), 1)
            V.tensor_copy(gdn_taps[:].rearrange("p a n -> p (a n)"), ps[:, 7, 16 + 8 * FC:16 + 8 * FC + P]).then_inc(S("cols_done"), 1)
            v.wait_ge(S("c_silu"), 1)
            V.tensor_copy(cond_bc[:], c_col[:].unsqueeze(2).broadcast_to([P, KD, P])).then_inc(S("cond_done"), 1)
            inv_root(stat[:, 0, 0:TT], D, EPS, TT)

            def mod(j):
                v.wait_ge(S("ada_used"), 4 * (j + 1))
                v.wait_ge(S("ada_b_in"), 16)
                V.tensor_tensor(mods[:, j, :], mods[:, j, :], bank2(2 * (j % 2)), ALU.add).then_inc(S("mods_done"), 1)
                v.wait_ge(S("mods_done"), j + 1)
                v.wait_ge(S("gains_in"), 16 * 5)
                if j in (1, 4):
                    V.scalar_tensor_tensor(mods[:, j, :], mods[:, j, :], 1.0, gains[:, PRE1 if j == 1 else PRE2, :],
                                           ALU.add, ALU.mult).then_inc(S("mods_gain"), 1)
                if j in (2, 5):
                    V.tensor_tensor(mods[:, j, :], mods[:, j, :], gains[:, POST1 if j == 2 else POST2, :], ALU.mult)\
                        .then_inc(S("mods_gain"), 1)

            mod(0)
            mod(1)
            v.wait_ge(S("mods_gain"), 1)
            for tt in range(TT):
                V.scalar_tensor_tensor(u_pool[:, tt, :], xres[:, tt, :], stat[:, 0, tt:tt + 1], mods[:, 1, :],
                                       ALU.mult, ALU.mult).then_inc(S("scaled"), 1)
                own("scaled")
                V.tensor_tensor(u_pool[:, tt, :], u_pool[:, tt, :], mods[:, 0, :], ALU.add).then_inc(S("u_ready"), 1)
            mod(2)
            mod(3)
            mod(4)
            v.wait_ge(S("mods_gain"), 3)
            for step in range(TT + 2):
                if step < TT:
                    v.wait_ge(S("y_mm"), step + 1)
                    V.tensor_tensor(y_pool[:, step, :], bank2(4 + 2 * (step % 2)), gains[:, PSCALE, :], ALU.mult)\
                        .then_inc(S("ys_done"), 1)
                if step >= 2:
                    tt = step - 2
                    inv_root(stat[:, 2, tt:tt + 1], D, EPS, TT + 2 * tt + 2)
                    if step == 2:
                        v.wait_ge(S("y_mm"), TT)
                    V.scalar_tensor_tensor(u_ffn[:, tt, :], xres[:, tt, :], stat[:, 2, tt:tt + 1], mods[:, 4, :],
                                           ALU.mult, ALU.mult).then_inc(S("scaled"), 1)
                    own("scaled")
                    V.tensor_tensor(u_ffn[:, tt, :], u_ffn[:, tt, :], mods[:, 3, :], ALU.add).then_inc(S("u2_ready"), 1)
                if 1 <= step <= TT:
                    tt = step - 1
                    inv_root(stat[:, 1, tt:tt + 1], D, EPS, TT + 2 * tt + 1)
                    V.scalar_tensor_tensor(y_pool[:, tt, :], y_pool[:, tt, :], stat[:, 1, tt:tt + 1], mods[:, 2, :],
                                           ALU.mult, ALU.mult).then_inc(S("scaled"), 1)
                    own("scaled")
                    V.tensor_tensor(xres[:, tt, :], xres[:, tt, :], y_pool[:, tt, :], ALU.add).then_inc(S("x1_done"), 1)
            mod(5)
            for tt in range(TT):
                parts_low(0, tt, 4 + 2 * (tt % 2))

            v.sem_inc(S("conv_done"), 4)
            v.sem_inc(S("act_done"), 2)
            with v.Fori(0, UP // 2) as i:
                for s in range(2):
                    for sub in range(2):
                        chunk = i * 2 + sub + s * FC
                        src, dst = ps[:, 2 * s + sub, :], conv_out[:, s, sub, :]
                        v.wait_ge(S("conv_mid"), i * 4 + 2 * s + sub + 1)
                        V.scalar_tensor_tensor(dst[:, 1:T], src[:, 0:T - 1], conv_taps[:, 0, ds(chunk, 1)], dst[:, 1:T],
                                               ALU.mult, ALU.add).then_inc(S("conv_left"), 1)
                        v.wait_ge(S("conv_left"), i * 4 + 2 * s + sub + 1)
                        V.scalar_tensor_tensor(dst[:, 0:T - 1], src[:, 1:T], conv_taps[:, 1, ds(chunk, 1)], dst[:, 0:T - 1],
                                               ALU.mult, ALU.add).then_inc(S("conv_done"), 1)
                        if s == 1:
                            v.wait_ge(S("conv_done"), i * 4 + 7 + sub)
                            v.wait_ge(S("gelu_done"), i * 2 + sub + 1)
                            V.tensor_tensor(acts[:, ds(i * 2 + sub, 1), :].rearrange("p a t -> p (a t)"),
                                            conv_out[:, 0, sub, :], conv_out[:, 1, sub, :], ALU.mult).then_inc(S("act_done"), 1)
            def act_parts(u):
                for kk in range(2):
                    k, slot = u * 2 + kk, (u % 2) * 2 + kk
                    if u >= 2:
                        v.wait_ge(w_used, U_DOWN + u - 1)
                    V.tensor_copy(act_parts_h[:, slot, :], acts[:, k, :]).then_inc(S("act_hi"), 1)
                    v.wait_ge(S("act_hi"), k + 1)
                    V.tensor_tensor(act_parts_l[:, slot, :], acts[:, k, :], act_parts_h[:, slot, :].bitcast(f32), ALU.subtract)\
                        .then_inc(S("act_split"), 1)

            v.wait_ge(S("act_done"), 2 + FC)
            for u in range(DOWN):
                act_parts(u)
            v.wait_ge(S("ba_in"), 16)
            V.tensor_copy(ba_h[:], ba_raw[:]).then_inc(S("ba_hi"), 1)
            v.wait_ge(S("ba_hi"), 1)
            V.tensor_tensor(ba_l[:], ba_raw[:], ba_h[:].bitcast(f32), ALU.subtract).then_inc(S("ba_split"), 1)
            for tt in range(TT):
                inv_root(stat[:, 3, tt:tt + 1], D, EPS, 3 * TT + tt + 1)
                V.scalar_tensor_tensor(f_scaled[:, tt, :], bank2(2 * tt), stat[:, 3, tt:tt + 1], mods[:, 5, :],
                                       ALU.mult, ALU.mult).then_inc(S("scaled"), 1)
                own("scaled")
                V.tensor_tensor(xres[:, tt, :], xres[:, tt, :], f_scaled[:, tt, :], ALU.add).then_inc(S("x2_done"), 1)
            for tt in range(TT):
                parts_low(1, tt, 2 * tt)

            ba = ps[:, 7, 0:TT * 2 * H].rearrange("p (t n) -> p t n", n=2 * H)
            v.wait_ge(S("ba_mm"), 1)
            v.wait_ge(S("alog_in"), 48)
            V.tensor_tensor(ba_tmp[:, 1], ba[:, :, H:2 * H], alog_dt[:, 1, :].unsqueeze(1).broadcast_to([P, TT, H]), ALU.add)\
                .then_inc(S("ba_z"), 1)
            V.tensor_copy(ba_tmp[:, 0], ba[:, :, 0:H]).then_inc(S("ba_z"), 1)
            v.wait_ge(S("ba_z"), 2)
            V.scalar_tensor_tensor(ba_tmp[:, 2], ba_tmp[:, 1], -1.0, ba_tmp[:, 1], ALU.mult, ALU.min).then_inc(S("ba_ready"), 1)
            v.wait_ge(S("ba_exp"), 4)
            V.tensor_scalar(ba_tmp[:, 0], ba_tmp[:, 0], 1.0, None, ALU.add).then_inc(S("ba_z"), 1)
            V.scalar_tensor_tensor(ba_tmp[:, 3], ba_tmp[:, 1], 0.0, ba_tmp[:, 2], ALU.max, ALU.add).then_inc(S("ba_z"), 1)
            v.wait_ge(S("ba_z"), 4)
            V.reciprocal(ba_tmp[:, 0], ba_tmp[:, 0]).then_inc(S("beta_done"), 1)
            V.scalar_tensor_tensor(scal[:, GLOG], ba_tmp[:, 3], -1.0, alog_dt[:, 0, :].unsqueeze(1).broadcast_to([P, TT, H]),
                                   ALU.mult, ALU.mult).then_inc(S("glog_done"), 1)

            def th(x):
                return x.rearrange("p (t h) -> p t h", h=H)

            def taps(n, s, sub):
                src, dst = ps[:, 2 * s + sub, :], conv_v[:, sub, :]
                v.wait_ge(S("tap3"), n + 1)
                for j in (1, 2, 3):
                    w = gdn_taps[:, 3 - j, ds(n, 1)] if not isinstance(n, int) else gdn_taps[:, 3 - j, n:n + 1]
                    if j > 1:
                        v.wait_ge(S("tap_mid"), n * 2 + j - 1)
                    V.scalar_tensor_tensor(dst[:, j:T], src[:, 0:T - j], w, dst[:, j:T], ALU.mult, ALU.add)\
                        .then_inc(S("qkv_conv") if j == 3 else S("tap_mid"), 1)

            def unit_taps(n, s):
                for sub in range(2):
                    taps(n * 2 + sub, s, sub)

            def values(h):
                v.wait_ge(S("v_turned"), h + 2)
                v.wait_ge(S("parts_lo"), 2 * TT)
                dst = val[:, :, h, :] if isinstance(h, int) else val[:, :, ds(h, 1), :].rearrange("p t a n -> p t (a n)")
                V.tensor_copy(dst, bank2(4).rearrange("p (t n) -> p t n", n=DV)).then_inc(S("val_done"), 1)

            qk_flat = qkt[:].rearrange("p a h t -> p (a h) t")

            def square(n, s):
                v.wait_ge(S("ss_mm"), n + 1)
                v.wait_ge(S("qk_silu"), n * 2 + 4)
                x = qk_flat[:, ds(n * 2, 2), :]
                V.tensor_tensor(squares[:, s], x, x, ALU.mult).then_inc(S("sq_done"), 1)

            v.sem_inc(S("qkv_conv"), 4)
            v.wait_ge(S("gc_mm"), 1)
            V.tensor_copy(scal[:, GC], th(ps[:, 7, 64:96])).then_inc(S("gc_copied"), 1)
            v.wait_ge(S("gc_copied"), 1)
            V.tensor_tensor(scal[:, KDS], th(ps[:, 7, 96:128]), scal[:, GC], ALU.subtract).then_inc(S("gc_ready"), 1)
            unit_taps(0, 0)
            square(0, 0)
            unit_taps(1, 1)
            square(1, 1)
            with v.Fori(1, GIN_QK // 2) as i:
                for s in range(2):
                    unit_taps(i * 2 + s, s)
                    square(i * 2 + s, s)
            unit_taps(GIN_QK, 0)
            with v.Fori(0, GIN_V // 2 - 1) as i:
                for s in range(2):
                    unit_taps(i * 2 + GIN_QK + 1 + s, 1 - s)
                    values(i * 2 + s)
            unit_taps(GIN_QK + GIN_V - 1, 1)
            values(GIN_V - 2)
            values(GIN_V - 1)
            sums = ps[:, 6, 0:2 * H * TT].rearrange("p (a h t) -> p a t h", a=2, t=TT)
            v.wait_ge(S("ss_mm"), 2 + GIN_QK)
            V.tensor_scalar(scal[:, RKI], sums[:, 1], EPS, None, ALU.add).then_inc(S("mean_done"), 1)
            V.tensor_scalar(scal[:, QS], sums[:, 0], EPS, None, ALU.add).then_inc(S("mean_done"), 1)
            with v.Fori(0, GIN_GATE // 2) as i:
                for s in range(2):
                    v.wait_ge(S("gate_silu"), i * 2 + s + 1)
                    g = gate[:, :, ds(i * 2 + s, 1), :].rearrange("p t a n -> p t (a n)")
                    V.tensor_tensor(g, g, norm_w[:].unsqueeze(1).broadcast_to([P, TT, DV]), ALU.mult).then_inc(S("gate_done"), 1)

            count = [0]

            def step(ins):
                count[0] += 1
                ins.then_inc(S("factors"), 1)
                v.wait_ge(S("factors"), count[0])

            roots[0] += 2
            v.wait_ge(S("root_done"), roots[0])
            v.wait_ge(S("gc_exp"), 3)
            v.wait_ge(S("beta_done"), 1)
            step(V.reciprocal(scal[:, RK], scal[:, RKI]))
            step(V.reciprocal(scal[:, QA], scal[:, QS]))
            step(V.tensor_scalar(scal[:, QS], scal[:, QA], KEY_SCALE, None, ALU.mult))
            step(V.scalar_tensor_tensor(scal[:, QA], scal[:, QA], KEY_SCALE * KEY_SCALE / DV, scal[:, QA], ALU.mult, ALU.mult))
            step(V.tensor_tensor(scal[:, VSC], ba_tmp[:, 0], scal[:, RK], ALU.mult))
            step(V.tensor_tensor(scal[:, BSC], scal[:, VSC], scal[:, RK], ALU.mult))
            step(V.tensor_tensor(scal[:, KEG], scal[:, KEG], scal[:, RK], ALU.mult))
            step(V.tensor_tensor(scal[:, KDS], scal[:, KDS], scal[:, RK], ALU.mult))

            v.wait_ge(S("state_zero"), 1)
            with v.Fori(0, TT) as i:
                tok = ds(i * P, P)
                V.tensor_copy(scal_now[:], scal[:, :, ds(i, 1), :].rearrange("p n a h -> p n (a h)")).then_inc(S("staged"), 1)
                V.tensor_copy(k_now[:], qkt[:, 1, :, tok]).then_inc(S("staged"), 1)
                v.wait_ge(S("staged"), i * 2 + 2)
                for g in range(2):
                    hs = slice(4 * g, 4 * g + 4)
                    v.wait_ge(S("eg_done"), i * 2 + g + 1)
                    for h in range(4 * g, 4 * g + 4):
                        dd = V.tensor_scalar(part[:, h, :], ps[:, 4 + g, (h % 4) * P:(h % 4 + 1) * P], scal_now[:, GC, h:h + 1], 0.0,
                                             ALU.subtract, ALU.min)
                    dd.then_inc(S("dec_diff"), 1)
                for g in range(2):
                    hs = slice(4 * g, 4 * g + 4)
                    v.wait_ge(S("eg_done"), i * 2 + g + 1)
                    V.tensor_tensor(q_dec[:, hs, :], qkt[:, 0, hs, tok], upper_m[:, hs, :], ALU.mult).then_inc(S("qdec_done"), 1)
                for g in range(2):
                    v.wait_ge(S("raw_mm"), i * 2 + g + 1)
                    v.wait_ge(S("dec_done"), i * 2 + g + 1)
                    for h in range(4 * g, 4 * g + 4):
                        b, o = 2 * g + (h % 4) // 2, (h % 2) * 2 * P
                        V.scalar_tensor_tensor(attn[:, h, :], ps[:, b, o:o + P], scal_now[:, RK, h:h + 1], part[:, h, :],
                                               ALU.mult, ALU.mult).then_inc(S("attn_done"), 1)
                        uu = V.scalar_tensor_tensor(upper[:, h, :], ps[:, b, o + P:o + 2 * P], scal_now[:, BSC, h:h + 1],
                                                    part[:, h, :], ALU.mult, ALU.mult)
                    uu.then_inc(S("u_done"), 1)
                v.wait_ge(S("ktok_mm"), i + 1)
                for g in range(2):
                    hs = slice(4 * g, 4 * g + 4)
                    v.wait_ge(S("um_done"), i * 14 + g + 1)
                    V.tensor_tensor(tri_inv[:, hs, :], ident[:].unsqueeze(1).broadcast_to([P, 4, P]), upper_m[:, hs, :],
                                    ALU.subtract).then_inc(S("y0_done"), 1)
                for l in range(1, LEVELS):
                    for g in range(2):
                        hs = slice(4 * g, 4 * g + 4)
                        v.wait_ge(S("xy_mm"), i * 12 + 2 * (l - 1) + g + 1)
                        if l < LEVELS - 1:
                            V.tensor_tensor(tri_inv_t[:, hs, :], tri_inv_t[:, hs, :],
                                            ps[:, 2 * g + 1, :].rearrange("p (h n) -> p h n", n=P), ALU.subtract)
                        V.tensor_tensor(tri_inv[:, hs, :], tri_inv[:, hs, :],
                                        ps[:, 4 + g, :].rearrange("p (h n) -> p h n", n=P), ALU.subtract).then_inc(S("xy_done"), 1)
                v.wait_ge(S("xy_done"), i * 12 + 12)
                for g in range(2):
                    for h in range(4 * g, 4 * g + 4):
                        yy = V.tensor_scalar(tri_inv[:, h, :], tri_inv[:, h, :], scal_now[:, RKI, h:h + 1], None, ALU.mult)
                    yy.then_inc(S("yfin_done"), 1)
                for g in range(2):
                    v.wait_ge(S("kin_done"), i * 2 + g + 1)
                    for h in range(4 * g, 4 * g + 4):
                        kd = V.tensor_scalar(k_dec[:, h, :], ps[:, 6 + g, (h % 4) * P:(h % 4 + 1) * P], scal_now[:, KDS, h:h + 1], None,
                                             ALU.mult)
                    kd.then_inc(S("kdec_done"), 1)
                for h in range(H):
                    v.wait_ge(S("vn_mm"), i * H + (h | 1) + 1)
                    V.tensor_scalar(val[:, ds(i, 1), h, :].rearrange("p a n -> p (a n)"),
                                    ps[:, (1, 3, 4, 5)[h // 2], (h % 2) * DV:(h % 2 + 1) * DV], scal_now[:, VSC, h:h + 1], None,
                                    ALU.mult).then_inc(S("vn_done"), 1)
                for h in range(H):
                    v.wait_ge(S("kv_mm"), i * H + (h | 1) + 1)
                    V.scalar_tensor_tensor(state[:, h, :], state[:, h, :], scal_now[:, GL, h:h + 1],
                                           ps[:, (1, 3, 4, 5)[h // 2], (h % 2) * DV:(h % 2 + 1) * DV], ALU.mult, ALU.add)\
                        .then_inc(S("s_done"), 1)
                v.wait_ge(S("o_ss"), i + 1)
                V.tensor_tensor(coef[:, 1, :], coef[:, 0, :], scal_now[:, QA, :], ALU.mult).then_inc(S("o_mean"), 1)
                v.wait_ge(S("o_mean"), i + 1)
                V.tensor_scalar(coef[:, 1, :], coef[:, 1, :], EPS, None, ALU.add).then_inc(S("o_ms"), 1)
                v.wait_ge(S("o_rt"), i + 1)
                V.reciprocal(coef[:, 2, :], coef[:, 1, :]).then_inc(S("o_inv"), 1)
                v.wait_ge(S("o_inv"), i * 2 + 1)
                V.tensor_tensor(coef[:, 3, :], coef[:, 2, :], scal_now[:, QS, :], ALU.mult).then_inc(S("o_inv"), 1)
                v.wait_ge(S("o_inv"), i * 2 + 2)
                for h in range(H):
                    V.scalar_tensor_tensor(gated_now[:, h, :], ps[:, (0, 2, 6, 7)[h // 2], (h % 2) * DV:(h % 2 + 1) * DV],
                                           coef[:, 3, h:h + 1], gate[:, ds(i, 1), h, :].rearrange("p a n -> p (a n)"),
                                           ALU.mult, ALU.mult).then_inc(S("og_done"), 1)
                for b in range(4):
                    v.wait_ge(S("ogt_hi"), i * 4 + b + 1)
                    V.tensor_tensor(ogt_l[:, ds(i, 1), 4 * b:4 * b + 4, :].rearrange("p a k n -> p (a k) n"),
                                    ps[:, (1, 3, 4, 5)[b], :].rearrange("p (k n) -> p k n", n=P),
                                    ogt_h[:, ds(i, 1), 4 * b:4 * b + 4, :].rearrange("p a k n -> p (a k) n").bitcast(f32),
                                    ALU.subtract).then_inc(S("ogt_lo"), 1)

            def layer_norm(stage, name, stats, mean_var):
                for tt in range(TT):
                    v.wait_ge(S("proj_mm"), stage * TT + tt + 1)
                    V.scalar_tensor_tensor(xres[:, tt, :], xres[:, tt, :], ALPHA, bank2(2 * tt), ALU.mult, ALU.add)\
                        .then_inc(S("ln_sum"), 1)
                    own("ln_sum")
                    for n in range(2):
                        V.bn_stats(stats[:, tt, n, :], xres[:, tt, n * 512:(n + 1) * 512]).then_inc(S("ln_stats"), 1)
                        own("ln_stats")
                    V.bn_aggr(mean_var[:, tt, :], stats[:, tt].rearrange("p a n -> p (a n)")).then_inc(S("ln_mean"), 1)
                    own("ln_mean")
                    V.tensor_scalar(mean_var[:, tt, 1:2], mean_var[:, tt, 1:2], LN_EPS, None, ALU.add).then_inc(S("mean_done"), 1)
                v.wait_ge(S(name + "_in"), 32)
                for tt in range(TT):
                    inverse(mean_var[:, tt, 1:2])
                    V.tensor_scalar(xres[:, tt, :], xres[:, tt, :], mean_var[:, tt, 0:1], mean_var[:, tt, 1:2],
                                    ALU.subtract, ALU.mult).then_inc(S("ln_norm"), 1)
                    own("ln_norm")
                    V.tensor_tensor(xres[:, tt, :], xres[:, tt, :], ln_gb[:, 0, :], ALU.mult).then_inc(S("ln_norm"), 1)
                    own("ln_norm")
                    V.tensor_tensor(xres[:, tt, :], xres[:, tt, :], ln_gb[:, 1, :], ALU.add).then_inc(S(name + "_done"), 1)

            layer_norm(1, "ln1", bn, mv)
            for tt in range(TT):
                parts_low(2, tt, 2 * tt)

            v.wait_ge(S("low_in"), 48)
            V.tensor_copy(low_h[:], low_raw[:]).then_inc(S("low_hi"), 1)
            v.wait_ge(S("low_hi"), 1)
            V.tensor_tensor(low_l[:], low_raw[:], low_h[:].bitcast(f32), ALU.subtract).then_inc(S("low_split"), 1)
            flat = "p h t -> p (h t)"
            V.memset(attn_g[:], 1.0).then_inc(S("reset_set"), 1)
            v.wait_ge(S("reset_set"), 1)
            V.memset(attn_g[:].rearrange("p h (t c) -> p h t c", c=P)[:, :, :, 0:1], 0.0).then_inc(S("reset_set"), 1)
            v.wait_ge(S("gk_z"), LH)
            V.scalar_tensor_tensor(eg[:], zg[:], -1.0, zg[:], ALU.mult, ALU.min).then_inc(S("gk_abs"), 1)
            v.wait_ge(S("gk_exp"), 2)
            V.scalar_tensor_tensor(eg[:], zg[:], 0.0, eg[:], ALU.min, ALU.subtract).then_inc(S("gk_log"), 1)
            v.wait_ge(S("gk_log"), 1)
            v.wait_ge(S("reset_set"), 2)
            V.tensor_tensor_scan(bg[:].rearrange(flat), attn_g[:].rearrange(flat), eg[:].rearrange(flat), 0.0, ALU.mult, ALU.add)\
                .then_inc(S("gk_sum"), 1)
            v.wait_ge(S("gk_sum"), 1)
            V.memset(attn_g[:], 0.0).then_inc(S("attn_zero"), 1)
            v.wait_ge(S("attn_zero"), 1)

            def merge(item):
                mask = (ident[:] if item == 0 else masks[:, item - 1, :]).bitcast(u32).unsqueeze(1).broadcast_to([P, TT, P])
                v.wait_ge(S("lev_mm"), item + 1)
                for h in range(LH):
                    mm = V.copy_predicated(attn_g[:, h, :].rearrange("p (t c) -> p t c", c=P), mask,
                                           ps[:, 4 + h, :].rearrange("p (t c) -> p t c", c=P))
                mm.then_inc(S("lev_merged"), 1)

            for l in range(LEVELS):
                n = 1 << l

                def halves(x):
                    return x[:].rearrange("p h t -> p (h t)").rearrange("p (b a n) -> p b a n", a=2, n=n)
                b4, e4, z4 = halves(bg), halves(eg), halves(zg)
                mid = b4[:, :, 0, n - 1:n].broadcast_to([P, LH * T // (2 * n), n])
                if l:
                    v.wait_ge(S("lev_z"), l)
                V.tensor_tensor(e4[:, :, 0, :], mid, b4[:, :, 0, :], ALU.subtract)
                V.tensor_tensor(e4[:, :, 1, :], b4[:, :, 1, :], mid, ALU.subtract).then_inc(S("lev_diff"), 1)
                merge(l)
                v.wait_ge(S("lqk_done"), LIN_QK)
                v.wait_ge(S("lev_exp"), l + 1)
                V.tensor_tensor(z4[:, :, 0, :], halves(kg)[:, :, 0, :], e4[:, :, 0, :], ALU.mult)
                V.tensor_tensor(z4[:, :, 1, :], halves(qg)[:, :, 1, :], e4[:, :, 1, :], ALU.mult).then_inc(S("lev_z"), 1)
            for j in range(LIN_GATE):
                v.wait_ge(S("lv_done"), LIN_V + j + 1)
                V.tensor_tensor(gg[:, :, j, :], gg[:, :, j, :], norm_w2[:].unsqueeze(1).broadcast_to([P, TT, DV]), ALU.mult)\
                    .then_inc(S("lgate_done"), 1)
            merge(LEVELS)
            v.wait_ge(S("qe_exp"), 2)
            V.tensor_tensor(zg[:], qg[:], eg[:], ALU.mult).then_inc(S("qe_done"), 1)
            b_chunk = bg[:].rearrange("p h (t c) -> p (h t) c", c=P)
            v.wait_ge(S("qe_done"), 1)
            V.tensor_tensor(eg[:].rearrange("p h (t c) -> p (h t) c", c=P), b_chunk[:, :, P - 1:P].broadcast_to([P, LH * TT, P]),
                            b_chunk, ALU.subtract).then_inc(S("kd_diff"), 1)
            v.wait_ge(S("kd_exp"), 1)
            V.tensor_tensor(eg[:], eg[:], kg[:], ALU.mult).then_inc(S("kd_scaled"), 1)
            v.wait_ge(S("kd_scaled"), 1)
            for tt in range(TT - 1):
                for h in range(LH):
                    n = tt * LH + h
                    v.wait_ge(S("lkv_mm"), (n | 1) + 1)
                    kv = ps[:, n // 2, (n % 2) * DV:(n % 2 + 1) * DV]
                    if tt == 0:
                        V.tensor_copy(states[:, 0, h, :], kv).then_inc(S("st_done"), 1)
                    else:
                        v.wait_ge(S("st_done"), n - LH + 1)
                        V.scalar_tensor_tensor(states[:, tt, h, :], states[:, tt - 1, h, :], glast_exp[:, h, tt:tt + 1], kv,
                                               ALU.mult, ALU.add).then_inc(S("st_done"), 1)
            for tt in range(TT):
                inv_root(stat[:, 4 + tt, 0:LH], DV, EPS, 4 * TT + (tt + 1) * LH)
                v.wait_ge(S("lgate_done"), LIN_GATE)
                for h in range(LH):
                    og = V.scalar_tensor_tensor(gg[:, tt, h, :], ps[:, O_BANK[tt] + h // 2, (h % 2) * DV:(h % 2 + 1) * DV],
                                                stat[:, 4 + tt, h:h + 1], gg[:, tt, h, :], ALU.mult, ALU.mult)
                og.then_inc(S("lo_gated"), 1)
            for tt in range(TT):
                parts_low(3, tt, O_BANK[tt])
            layer_norm(2, "ln2", bn2, mv2)

        @block.tensor
        def _(pe):
            X = nc.tensor

            def turn(o, x, n=P):
                return X.transpose(o, x, ident[0:n, 0:n])

            pe.wait_ge(S("c_in"), 16)
            pe.wait_ge(S("rows_in"), 16 * 5)
            pe.wait_ge(S("ident_in"), 16)
            turn(ps[:, 6, 0:KD + LH], rows[0:KD + LH, 0, :], KD + LH)
            turn(ps[:, 7, 16:16 + 4 * FC], rows[0:4 * FC, 1, :], 4 * FC)
            turn(ps[:, 7, 16 + 4 * FC:16 + 8 * FC], rows[0:4 * FC, 2, :], 4 * FC)
            turn(ps[:, 7, 16 + 8 * FC:16 + 8 * FC + P], rows[:, 3, :]).then_inc(S("rows_turned"), 1)

            def mod(j):
                if j >= 2:
                    pe.wait_ge(S("mods_done"), j - 1)
                for n in range(4):
                    pe.wait_ge(ada_full[n], 16 * (j + 1))
                    o = ps[:, 2 * (j % 2) + n // 2, (n % 2) * UC:(n % 2 + 1) * UC]
                    for k in range(KD):
                        mm = X.matmul(o, cond_bc[:, k, :], ada[:, n, k, :], start=(k == 0), stop=(k == KD - 1))
                    mm.then_inc(S("ada_used"), 1)

            pe.wait_ge(S("cond_done"), 1)
            mod(0)
            mod(1)
            mod(2)
            pe.wait_ge(S("pool_in"), 32)
            pe.wait_ge(S("cols_done"), 3)
            for cb in range(KD):
                if cb >= 4:
                    pe.wait_ge(S("pooled_done"), cb - 3)
                for tt in range(TT):
                    pe.wait_ge(S("u_ready"), tt + 1)
                    c0, nc_ = band_start(tt), band_cols(tt)
                    mm = X.matmul(ps[:, 4 + cb % 4, c0:c0 + nc_], u_pool[:, tt, cb * P:(cb + 1) * P],
                                  pool_band[:, cb // 2, tt, 0:nc_], start=(tt == 0), stop=(tt == TT - 1), skip_group_check=True)
                mm.then_inc(S("pool_mm"), 1)
            mod(3)
            mod(4)
            pe.wait_ge(S("pooled_done"), KD)
            for tt in range(TT):
                if tt >= 2:
                    pe.wait_ge(S("ys_done"), tt - 1)
                for g in range(POOL_GROUPS):
                    for k in range(2):
                        mm = X.matmul(ps[:, 4 + 2 * (tt % 2) + g // 2, (g % 2) * GDIM:(g % 2 + 1) * GDIM],
                                      pooled[:, 2 * g + k, tt * P:(tt + 1) * P], pool_w[:, g, k, :], start=(k == 0), stop=(k == 1))
                mm.then_inc(S("y_mm"), 1)
            mod(5)

            def turn_tile(x, b):
                for k in range(KD):
                    mm = turn(ps[:, b + k // 4, (k % 4) * P:(k % 4 + 1) * P], x[:, k * P:(k + 1) * P])
                mm.then_inc(S("turned"), 1)

            pe.wait_ge(S("ys_done"), TT)
            for tt in range(TT):
                if tt >= 2:
                    pe.wait_ge(S("parts_lo"), tt - 1)
                pe.wait_ge(S("u2_ready"), tt + 1)
                turn_tile(u_ffn[:, tt, :], 4 + 2 * (tt % 2))

            def col_chunk(slot, sub, o):
                whk = wh[:, slot, :].rearrange("p (k n) -> p k n", n=UC)
                wlk = wl[:, slot, :].rearrange("p (k n) -> p k n", n=UC)
                c = slice(sub * P, (sub + 1) * P)
                for k in range(KD):
                    mm = mm3(o, whk[:, k, c], wlk[:, k, c], xth[:, k, :], xtl[:, k, :], k == 0, k == KD - 1)
                return mm

            pe.wait_ge(S("parts_lo"), 1 * TT)
            pe.wait_ge(S("mods_done"), 6)
            with pe.Fori(0, UP // 2) as i:
                for s in range(2):
                    pe.wait_ge(unit_split, i * 2 + s + 1)
                    for sub in range(2):
                        pe.wait_ge(S("conv_done"), i * 4 + 2 * s + sub + 1)
                        col_chunk(s, sub, ps[:, 2 * s + sub, :]).then_inc(S("up_half") if sub == 0 else w_used, 1)

            def down_unit(stage, u0, n, lh, ll, ready):
                for u in range(n):
                    slot = (u0 + u) % 2
                    whk = wh[:, slot, :].rearrange("p (k n) -> p k n", n=D)
                    wlk = wl[:, slot, :].rearrange("p (k n) -> p k n", n=D)
                    pe.wait_ge(unit_split, u0 + u + 1)

                    def product(tt, half, kk):
                        k = 2 * u + kk
                        c = slice(half * 512, half * 512 + 512)
                        return mm3(ps[:, 2 * tt + half, :], lh(k, tt), ll(k, tt), whk[:, kk, c], wlk[:, kk, c],
                                   k == 0, k == 2 * n - 1)
                    if u < n - 1:
                        for kk in range(2):
                            ready(2 * u + kk)
                            for tt in range(TT):
                                for half in range(2):
                                    mm = product(tt, half, kk)
                        mm.then_inc(w_used, 1)
                    else:
                        ready(2 * u + 1)
                        for tt in range(TT):
                            for half in range(2):
                                for kk in range(2):
                                    mm = product(tt, half, kk)
                            mm.then_inc(S("proj_mm"), 1)
                        pe.wait_ge(S("proj_mm"), (stage + 1) * TT)
                        pe.sem_inc(w_used, 1)

            pe.wait_ge(S("conv_done"), 4 + 2 * FC)
            down_unit(0, U_DOWN, DOWN, lambda k, tt: act_parts_h[:, k % 4, tt * P:(tt + 1) * P],
                      lambda k, tt: act_parts_l[:, k % 4, tt * P:(tt + 1) * P], 
                      lambda k: pe.wait_ge(S("act_split"), k + 1))
            for tt in range(TT):
                pe.wait_ge(S("x2_done"), tt + 1)
                turn_tile(xres[:, tt, :], 2 * tt)

            pe.wait_ge(S("parts_lo"), 2 * TT)
            pe.wait_ge(S("ba_split"), 1)
            for tt in range(TT):
                for k in range(KD):
                    mm = mm3(ps[:, 7, tt * 2 * H:(tt + 1) * 2 * H], xth[:, k, tt * P:(tt + 1) * P], xtl[:, k, tt * P:(tt + 1) * P],
                             ba_h[:, k, :], ba_l[:, k, :], k == 0, k == KD - 1)
            mm.then_inc(S("ba_mm"), 1)

            def qkv_unit(n, s):
                pe.wait_ge(unit_split, n + U_GIN + 1)
                for sub in range(2):
                    pe.wait_ge(S("qkv_conv"), n * 2 + sub + 1)
                    col_chunk((U_GIN + s) % 2, sub, ps[:, 2 * s + sub, :]).then_inc(S("qkv_half") if sub == 0 else w_used, 1)

            def sums(n, s):
                pe.wait_ge(S("sq_done"), n + 1)
                for sub in range(2):
                    for tt in range(TT):
                        c = (n * 2 + sub) * TT + tt
                        o = ps[:, 6, c:c + 1] if isinstance(c, int) else ps[:, 6, ds(c, 1)]
                        mm = X.matmul(o, squares[:, s, sub, tt * P:(tt + 1) * P], ones[:, 0:1], start=True, stop=True)
                mm.then_inc(S("ss_mm"), 1)

            def turn_values(h):
                pe.wait_ge(S("v_silu"), h * 2 + 2)
                pe.wait_ge(S("val_done"), h + 1)
                for tt in range(TT):
                    for sub in range(2):
                        b, o = 4 + tt // 2, (tt % 2) * DV + sub * P
                        mm = turn(ps[:, b, o:o + P], conv_v[:, sub, tt * P:(tt + 1) * P])
                mm.then_inc(S("v_turned"), 1)

            pe.sem_inc(S("ss_mm"), 2)
            pe.sem_inc(S("v_turned"), 1)
            pe.sem_inc(S("val_done"), 1)
            qkv_unit(0, 0)
            pe.wait_ge(S("glog_done"), 1)
            pe.wait_ge(S("masks_in"), 32)
            pe.wait_ge(S("ones_set"), 1)
            glog = scal[:, GLOG].rearrange("p t h -> p (t h)")
            X.matmul(ps[:, 7, 64:96], tri[:], glog, start=True, stop=True)
            X.matmul(ps[:, 7, 96:128], ones[:, 0:1].broadcast_to([P, P]), glog, start=True, stop=True).then_inc(S("gc_mm"), 1)
            with pe.Fori(0, GIN_QK // 2 - 1) as i:
                for s in range(2):
                    qkv_unit(i * 2 + 1 + s, 1 - s)
                    sums(i * 2 + s, s)
            qkv_unit(GIN_QK - 1, 1)
            sums(GIN_QK - 2, 0)
            qkv_unit(GIN_QK, 0)
            sums(GIN_QK - 1, 1)
            with pe.Fori(0, GIN_V // 2 - 1) as i:
                for s in range(2):
                    qkv_unit(i * 2 + GIN_QK + 1 + s, 1 - s)
                    turn_values(i * 2 + s)
            qkv_unit(GIN_QK + GIN_V - 1, 1)
            turn_values(GIN_V - 2)

            def token_unit(slot, b):
                whk = wh[:, slot, :].rearrange("p (k n) -> p k n", n=UC)
                wlk = wl[:, slot, :].rearrange("p (k n) -> p k n", n=UC)
                for tt in range(TT):
                    o = ps[:, b + tt // 2, (tt % 2) * UC:(tt % 2 + 1) * UC]
                    c = slice(tt * P, (tt + 1) * P)
                    for k in range(KD):
                        mm = mm3(o, xth[:, k, c], xtl[:, k, c], whk[:, k, :], wlk[:, k, :], k == 0, k == KD - 1)
                mm.then_inc(w_used, 1)

            u0 = U_GIN + GIN_QK + GIN_V
            for n in range(2):
                pe.wait_ge(unit_split, u0 + n + 1)
                pe.wait_ge(S("qkv_conv"), 4 + 2 * (GIN_QK + GIN_V) - 2 + 2 * n)
                token_unit((u0 + n) % 2, 2 * n)
                if n == 0:
                    turn_values(GIN_V - 1)
            with pe.Fori(1, GIN_GATE // 2) as i:
                for s in range(2):
                    pe.wait_ge(unit_split, i * 2 + u0 + s + 1)
                    pe.wait_ge(S("gate_silu"), i * 2 + s - 1)
                    token_unit((u0 + s) % 2, 2 * s)

            with pe.Fori(0, TT) as i:
                tok = ds(i * P, P)

                def head(b, h):
                    return ps[:, b, (h % 4) * P:(h % 4 + 1) * P]

                def half(banks, h):
                    return ps[:, banks[h // 2], (h % 2) * DV:(h % 2 + 1) * DV]

                pe.wait_ge(S("staged"), i * 2 + 2)
                for g in range(2):
                    for h in range(4 * g, 4 * g + 4):
                        mm = X.matmul(head(4 + g, h), scal_now[:, GLOG, h:h + 1].broadcast_to([P, P]), tri[:], start=True, stop=True)
                    mm.then_inc(S("gcrow_mm"), 1)
                for g in range(2):
                    for h in range(4 * g, 4 * g + 4):
                        b, o = 2 * g + (h % 4) // 2, (h % 2) * 2 * P
                        mm = X.matmul(ps[:, b, o:o + 2 * P], k_now[:, h, :], qkt[:, :, h, tok], start=True, stop=True)
                    mm.then_inc(S("raw_mm"), 1)
                for h in range(H):
                    mm = turn(head(6 + h // 4, h), k_now[:, h, :])
                mm.then_inc(S("ktok_mm"), 1)
                for g in range(2):
                    pe.wait_ge(S("y0_done"), i * 2 + g + 1)
                    for h in range(4 * g, 4 * g + 4):
                        mm = turn(head(2 * g, h), tri_inv[:, h, :])
                    mm.then_inc(S("x0_mm"), 1)
                for l in range(1, LEVELS):
                    for g in range(2):
                        pe.wait_ge(S("um_done"), i * 14 + 2 * l + g + 1)
                        if l == 1:
                            pe.wait_ge(S("x0_done"), i * 2 + g + 1)
                        else:
                            pe.wait_ge(S("xy_done"), i * 12 + 2 * (l - 2) + g + 1)
                        for h in range(4 * g, 4 * g + 4):
                            mm = X.matmul(head(2 * g, h), upper_m[:, h, :], tri_inv_t[:, h, :], start=True, stop=True)
                        mm.then_inc(S("p1_mm"), 1)
                    for g in range(2):
                        pe.wait_ge(S("p1_done"), i * 12 + 2 * (l - 1) + g + 1)
                        for h in range(4 * g, 4 * g + 4):
                            if l < LEVELS - 1:
                                X.matmul(head(2 * g + 1, h), tri_inv[:, h, :], part[:, h, :], start=True, stop=True)
                            mm = X.matmul(head(4 + g, h), part[:, h, :], tri_inv[:, h, :], start=True, stop=True)
                        mm.then_inc(S("xy_mm"), 1)
                for g in range(2):
                    pe.wait_ge(S("yfin_done"), i * 2 + g + 1)
                    pe.wait_ge(S("kin_done"), i * 2 + g + 1)
                    for h in range(4 * g, 4 * g + 4):
                        mm = X.matmul(head(2 * g, h), k_in[:, h, :], tri_inv[:, h, :], start=True, stop=True)
                    mm.then_inc(S("w_mm"), 1)
                for h in range(H):
                    o = half((1, 3, 4, 5), h)
                    if h % 4 == 0:
                        pe.wait_ge(S("w_done"), i * 2 + h // 4 + 1)
                    X.matmul(o, tri_inv[:, h, :], val[:, ds(i, 1), h, :].rearrange("p a n -> p (a n)"), start=True, stop=False)
                    X.matmul(o, part[:, h, :], state[:, h, :], start=False, stop=True).then_inc(S("vn_mm"), 1)
                for h in range(H):
                    if h % 4 == 0:
                        pe.wait_ge(S("kdec_done"), i * 2 + 2)
                    pe.wait_ge(S("vn_done"), i * H + (h | 1) + 1)
                    o = half((0, 2, 6, 7), h)
                    vn = val[:, ds(i, 1), h, :].rearrange("p a n -> p (a n)")
                    X.matmul(o, q_dec[:, h, :], state[:, h, :], start=True, stop=False)
                    X.matmul(o, attn[:, h, :], vn, start=False, stop=True).then_inc(S("o_mm"), 1)
                    X.matmul(half((1, 3, 4, 5), h), k_dec[:, h, :], vn, start=True, stop=True).then_inc(S("kv_mm"), 1)
                pe.wait_ge(S("s_done"), i * H + H)
                for b in range(4):
                    pe.wait_ge(S("og_done"), i * H + 2 * b + 2)
                    for k in range(4):
                        n = 4 * b + k
                        mm = turn(ps[:, (1, 3, 4, 5)[b], k * P:(k + 1) * P], gated_now[:, n // 2, (n % 2) * P:(n % 2 + 1) * P])
                    mm.then_inc(S("og_turned"), 1)

            pe.wait_ge(S("ogt_lo"), 4 * TT)
            down_unit(1, U_GOUT, GOUT, lambda k, tt: ogt_h[:, tt, k, :], lambda k, tt: ogt_l[:, tt, k, :], lambda k: None)
            for tt in range(TT):
                pe.wait_ge(S("ln1_done"), tt + 1)
                turn_tile(xres[:, tt, :], 2 * tt)

            pe.wait_ge(S("parts_lo"), 3 * TT)
            pe.wait_ge(S("low_split"), 1)
            for k in range(KD):
                mm = mm3(ps[0:16, 0, :], low_h[:, k, :], low_l[:, k, :], xth[:, k, :], xtl[:, k, :], k == 0, k == KD - 1)
            mm.then_inc(S("low_mm"), 1)
            for j in range(LIN_QK):
                u, b = U_LIN + j, 2 * (j % 2)
                pe.wait_ge(unit_split, u + 1)
                if j == 0:
                    pe.wait_ge(S("gk_low_done"), 1)
                if j >= 2:
                    pe.wait_ge(S("lqk_done"), j - 1)
                col_chunk(u % 2, 0, ps[:, b, :])
                col_chunk(u % 2, 1, ps[:, b + 1, :]).then_inc(w_used, 1)
                if j == 0:
                    for h in range(LH):
                        X.matmul(ps[:, 4 + h, :], gk_up[0:16, h * DK:(h + 1) * DK], gk_low[0:16, :], start=True, stop=True)\
                            .then_inc(S("gk_mm"), 1)
            for j in range(LIN_V + LIN_GATE):
                u, b = U_LIN + LIN_QK + j, 2 * (j % 2)
                pe.wait_ge(unit_split, u + 1)
                if j < 2:
                    pe.wait_ge(S("lqk_done"), LIN_QK - 1 + j)
                else:
                    pe.wait_ge(S("lv_done"), j - 1)
                token_unit(u % 2, b)
                if j == 0:
                    pe.wait_ge(S("lqk_done"), LIN_QK)
                    pe.wait_ge(S("gk_z"), LH)
                else:
                    pe.wait_ge(S("lev_merged"), j)
                    pe.wait_ge(S("lev_z"), j)
                for h in range(LH):
                    for tt in range(TT):
                        c = slice(tt * P, (tt + 1) * P)
                        mm = X.matmul(ps[:, 4 + h, c], (kg if j == 0 else zg)[:, h, c], (qg if j == 0 else zg)[:, h, c],
                                      start=True, stop=True)
                mm.then_inc(S("lev_mm"), 1)
            pe.wait_ge(S("lev_merged"), LEVELS + 1)
            pe.wait_ge(S("kd_scaled"), 1)
            for h in range(LH):
                for tt in range(TT):
                    mm = turn(ps[:, 4 + h, tt * P:(tt + 1) * P], eg[:, h, tt * P:(tt + 1) * P])
                mm.then_inc(S("kd_turned"), 1)
            pe.wait_ge(S("lv_done"), LIN_V + LIN_GATE)
            pe.wait_ge(S("kd_done"), LH)
            for tt in range(TT - 1):
                for h in range(LH):
                    n = tt * LH + h
                    X.matmul(ps[:, n // 2, (n % 2) * DV:(n % 2 + 1) * DV], kd_tok[:, h, tt, :], vg[:, tt, h, :], start=True, stop=True)\
                        .then_inc(S("lkv_mm"), 1)
            for tt in range(TT):
                if tt >= 1:
                    pe.wait_ge(S("st_done"), tt * LH)
                for h in range(LH):
                    c = slice(tt * P, (tt + 1) * P)
                    o = ps[:, O_BANK[tt] + h // 2, (h % 2) * DV:(h % 2 + 1) * DV]
                    mm = X.matmul(o, attn_g[:, h, c], vg[:, tt, h, :], start=True, stop=(tt == 0))
                    if tt >= 1:
                        mm = X.matmul(o, zg[:, h, c], states[:, tt - 1, h, :], start=False, stop=True)
                    mm.then_inc(S("lo_mm"), 1)
            for tt in range(TT):
                pe.wait_ge(S("lo_gated"), tt + 1)
                turn_tile(gg[:, tt].rearrange("p h n -> p (h n)"), O_BANK[tt])
            pe.wait_ge(S("parts_lo"), 4 * TT)
            down_unit(2, U_LOUT, LOUT, lambda k, tt: xth[:, k, tt * P:(tt + 1) * P], lambda k, tt: xtl[:, k, tt * P:(tt + 1) * P],
                      lambda k: None)


def constants():
    import numpy as np
    s, c = np.arange(P)[:, None], np.arange(P)[None, :]
    parts = [s == c, s <= c]
    for l in range(LEVELS):
        n = 1 << l
        parts.append((s // (2 * n) == c // (2 * n)) & (s // n % 2 == 0) & (c // n % 2 == 1))
    consts = np.concatenate(parts, axis=1).astype(np.float32)
    band = np.zeros((P, POOL_GROUPS, TT, BAND), np.float32)
    for g, w in enumerate(POOL_WINDOWS):
        m = np.zeros((T, T), np.float32)
        for t in range(T):
            lo, hi = max(t - w // 2, 0), min(t + w // 2, T)
            m[lo:hi, t] = np.float32(1.0) / np.float32(hi - lo)
            m[t, t] -= np.float32(1.0)
        for tt in range(TT):
            band[:, g, tt, :band_cols(tt)] = m[tt * P:(tt + 1) * P, band_start(tt):band_start(tt) + band_cols(tt)]
    return {"consts": consts, "pool_band": band.reshape(P, -1)}


INPUTS = ["x", "c", "ada_w", "ada_b", "mix_pre_g", "mix_post_g", "ffn_pre_g", "ffn_post_g", "pool_w", "pool_scale",
          "ffn_w_up", "ffn_conv_w", "ffn_conv_b", "ffn_w_down",
          "gdn_w_in_2", "gdn_conv_w_2", "gdn_a_log_2", "gdn_dt_bias_2", "gdn_norm_w_2", "gdn_w_out_2",
          "gla_w_in_2", "gla_w_gk_up_2", "gla_b_gk_2", "gla_norm_w_2", "gla_w_out_2", "ln_g_2", "ln_b_2"]


def kernel(**inputs):
    import numpy as np
    import concourse.bacc as bacc
    from concourse.bass_utils import run_bass_kernel_spmd as run

    nc = bacc.Bacc("TRN2", target_bir_lowering=False, num_devices=1)
    arrays = {n: np.ascontiguousarray(inputs[n]) for n in INPUTS}
    arrays.update(constants())
    aps = {n: nc.dram_tensor("in_" + n, x.shape, mybir.dt.from_np(x.dtype), kind="ExternalInput").ap()
           for n, x in arrays.items()}
    out = nc.dram_tensor("out", (1, T, D), mybir.dt.float32, kind="ExternalOutput").ap()
    build(nc, aps, out)
    result = run(nc, [{"in_" + n: x for n, x in arrays.items()}], core_ids=[0])
    return result.results[0]["out"]
```

```python
import concourse.bass as bass
from concourse import mybir
from concourse.alu_op_type import AluOpType as ALU
from contextlib import ExitStack

P = 128
T, D = 512, 1024
TT, KD = T // P, D // P
DFF = 2816
FC = DFF // P
POOL_GROUPS, POOL_WINDOWS = 4, (2, 4, 8, 16)
GDIM = D // POOL_GROUPS
BAND = P + 16
H, DK, DV = 8, 128, 256
LH = 4
UNIT = 2048
UC = UNIT // KD
LEVELS = 7
EPS, LN_EPS = 1e-6, 1e-5
ALPHA = 4.0 ** 0.25
GATE_NORM = 16.0
KEY_SCALE = DK ** -0.5

UP, DOWN = 2 * DFF // UC, DFF // (UNIT // D * P)
U_UP, U_DOWN = 0, UP
U_GIN = U_DOWN + DOWN
GIN_QK, GIN_V, GIN_GATE = 2 * H * DK // UC, H * DV // UC, H * DV // UC
U_GOUT = U_GIN + GIN_QK + GIN_V + GIN_GATE
GOUT = H * DV // (2 * P)
U_LIN = U_GOUT + GOUT
LIN_QK, LIN_V, LIN_GATE = 2 * LH * DK // UC, LH * DV // UC, LH * DV // UC
U_LOUT = U_LIN + LIN_QK + LIN_V + LIN_GATE
LOUT = LH * DV // (2 * P)
UNITS = U_LOUT + LOUT

ADA = 6 * D // UC
NORM_ORDER = (("y", 0), ("y", 1), ("y", 2), ("u", 0), ("y", 3), ("u", 1), ("u", 2), ("u", 3))
NSCAL = 11
O_BANK = (6, 0, 2, 4)
GC, BSC, RK, RKI, KEG, KDS, VSC, GL, QA, QS, GLOG = range(NSCAL)


def band_start(tt):
    return max(P * tt - 8, 0)


def band_cols(tt):
    return min(P * tt + P + 8, T) - band_start(tt)


def build(nc, a, out, debug=None):
    f32, f32r, u32 = mybir.dt.float32, mybir.dt.float32r, mybir.dt.uint32
    ACT = mybir.ActivationFunctionType
    KB = 1024
    ds = bass.ds

    BASE = 16640
    CONST, RAW0 = BASE, BASE + 7680
    WH0 = RAW0 + 16 * KB
    WL0 = WH0 + 16 * KB
    XRES0 = WL0 + 16 * KB
    XTH0 = XRES0 + 16 * KB
    XTL0 = XTH0 + 16 * KB
    PH = XTL0 + 16 * KB

    def at(name, offset, shape, dt=f32):
        return nc.alloc_sbuf_tensor_at(name, [P, *shape], dt, offset=offset)

    ident = at("ident", CONST, [P])
    tri = at("tri", CONST + 512, [P])
    masks = at("masks", CONST + 1024, [LEVELS, P])
    conv_taps = at("conv_taps", CONST + 4608, [2, 2 * 2 * FC])
    scal_now = at("scal_now", CONST + 4608, [NSCAL, H])
    gdn_taps = at("gdn_taps", CONST + 5312, [4, 4 * KD])
    ones = at("ones", CONST + 5824, [8])
    c_col = at("c_col", CONST + 5856, [KD])
    bgk_col = at("bgk_col", CONST + 5888, [LH])
    scal = at("scal", CONST + 5920, [NSCAL, TT, H])
    stat = at("stat", CONST + 7328, [8, 8])
    glast_exp = at("glast_exp", CONST + 7584, [LH, TT])

    raw = at("raw", RAW0, [2, UNIT])
    wh = at("wh", WH0, [2, UNIT], f32r)
    wl = at("wl", WL0, [2, UNIT], f32r)

    xres = at("xres", XRES0, [TT, D])
    xth = at("xth", XTH0, [KD, T], f32r)
    xtl = at("xtl", XTL0, [KD, T], f32r)

    u_pool = at("u_pool", XTH0, [TT, D])
    y_pool = at("y_pool", XTH0, [TT, D])
    rows = at("rows", XTL0, [4, P])
    pooled = at("pooled", XTL0, [KD, T])
    mods = at("mods", PH, [6, D])
    gains = at("gains", PH + 24 * KB, [5, D])
    PRE1, POST1, PRE2, POST2, PSCALE = range(5)
    partial = at("partial", PH + 44 * KB, [2, 2, UC])
    ada_rows = at("ada_rows", PH + 103 * KB, [UC])
    ada = at("ada", PH + 48 * KB, [4, KD, UC])
    pool_w = at("pool_w", PH + 80 * KB, [POOL_GROUPS, GDIM // P, GDIM])
    pool_band = at("pool_band", PH + 88 * KB, [POOL_GROUPS, TT, BAND])
    u_ffn = at("u_ffn", PH + 80 * KB, [TT, D])
    junk = at("junk", PH + 99 * KB, [D])

    conv_out = at("conv_out", PH, [2, 2, T])
    act_parts_h = at("act_parts_h", PH + 24 * KB, [4, T], f32r)
    act_parts_l = at("act_parts_l", PH + 32 * KB, [4, T], f32r)
    acts = at("acts", PH + 48 * KB, [FC, T])
    f_scaled = at("f_scaled", PH + 48 * KB, [TT, D])

    qkt = at("qkt", PH, [2, H, T])
    val = at("val", PH + 32 * KB, [TT, H, DV])
    gate = at("gate", PH + 64 * KB, [TT, H, DV])
    squares = at("squares", PH + 32 * KB, [2, 2, T])
    ba_raw = at("ba_raw", PH + 97 * KB, [KD, 2 * H])
    ba_h = at("ba_h", PH + 97 * KB + 512, [KD, 2 * H], f32r)
    ba_l = at("ba_l", PH + 97 * KB + 1024, [KD, 2 * H], f32r)
    ba_cols = at("ba_cols", PH + 64 * KB, [T])
    ba_tmp = at("ba_tmp", PH + 97 * KB + 1536, [4, TT, H])
    norm_w = at("norm_w", PH + 96 * KB, [DV])
    alog_dt = at("alog_dt", PH + 99 * KB, [2, H])
    conv_v = at("conv_v", PH + 100 * KB, [2, T])
    state = at("state", PH + 96 * KB, [H, DV])
    D0 = XTH0
    tri_inv = at("tri_inv", D0, [H, P])
    k_now = at("k_now", D0, [H, P])
    tri_inv_t = at("tri_inv_t", D0 + 4 * KB, [H, P])
    k_dec = at("k_dec", D0 + 4 * KB, [H, P])
    upper = at("upper", D0 + 8 * KB, [H, P])
    k_in = at("k_in", D0 + 8 * KB, [H, P])
    upper_m = at("upper_m", D0 + 12 * KB, [H, P])
    gated_now = at("gated_now", D0 + 8 * KB, [H, DV])
    part = at("part", D0 + 16 * KB, [H, P])
    attn = at("attn", D0 + 20 * KB, [H, P])
    q_dec = at("q_dec", D0 + 24 * KB, [H, P])
    prod = at("prod", D0 + 28 * KB, [H, P])
    coef = at("coef", CONST + 4960, [4, H])
    ogt_h = at("ogt_h", PH + 32 * KB, [TT, 2 * H, P], f32r)
    ogt_l = at("ogt_l", PH + 64 * KB, [TT, 2 * H, P], f32r)
    ln_gb = at("ln_gb", PH + 96 * KB, [2, D])
    mv = at("mv", PH + 17 * KB, [TT, 2])
    junk_ln = at("junk_ln", PH + 24 * KB, [D])

    qg = at("qg", PH, [LH, T])
    kg = at("kg", PH + 8 * KB, [LH, T])
    bg = at("bg", PH + 16 * KB, [LH, T])
    vg = at("vg", PH + 24 * KB, [TT, LH, DV])
    gg = at("gg", PH + 40 * KB, [TT, LH, DV])
    eg = at("eg", PH + 56 * KB, [LH, T])
    zg = at("zg", PH + 64 * KB, [LH, T])
    attn_g = at("attn_g", PH + 72 * KB, [LH, T])
    kd_chan = at("kd_chan", PH + 80 * KB, [LH, T])
    kd_tok = at("kd_tok", PH + 80 * KB, [LH, TT, P])
    norm_w2 = at("norm_w2", PH + 88 * KB, [DV])
    low_raw = at("low_raw", PH + 89 * KB, [KD, 16])
    low_h = at("low_h", PH + 89 * KB + 512, [KD, 16], f32r)
    low_l = at("low_l", PH + 90 * KB, [KD, 16], f32r)
    gk_up = at("gk_up", PH + 91 * KB, [LH * DK])
    gk_low = at("gk_low", PH + 93 * KB, [T])
    junk_g = at("junk_g", PH + 95 * KB, [DV])
    states = at("states", PH, [TT - 1, LH, DV])

    with ExitStack() as ctx:
        ps = ctx.enter_context(nc.psum_tensor("ps", [P, 8, 512], f32))
        made = {}

        def S(name):
            if name not in made:
                made[name] = ctx.enter_context(nc.semaphore(name))
            return made[name]

        raw_full = [S("raw_full0"), S("raw_full1")]
        hi_done = S("hi_done")
        unit_split = S("unit_split")
        w_used = S("w_used")
        ada_full = [S(f"ada_full{s}") for s in range(4)]

        def bank2(b):
            return ps[:, b:b + 2, :].rearrange("p b n -> p (b n)")

        def heads4(b):
            return ps[:, b, :].rearrange("p (h n) -> p h n", n=P)

        def halves(x, l, side):
            return x.rearrange("p h (b a n) -> p h b a n", a=2, n=1 << l)[:, :, :, side, :]

        def mm3(o, lh, ll, rh, rl, first, last):
            nc.tensor.matmul(o, lh, rh, start=first, stop=False)
            nc.tensor.matmul(o, lh, rl, start=False, stop=False)
            return nc.tensor.matmul(o, ll, rh, start=False, stop=last)

        block = ctx.enter_context(nc.Block())

        @block.sync
        def _(sp):
            def unit(u, src):
                slot, view = src
                sp.dma_start(raw[:, slot, :].rearrange("p (k n) -> p k n", k=view.shape[1]), view)\
                    .then_inc(raw_full[slot], 16)

            def cols(w, n):
                return w.rearrange("(k p) (u n) -> u p k n", p=P, n=n)

            def one(view, u):
                return view[ds(u, 1)].rearrange("a p k n -> p (a k) n")

            ada_v = cols(a["ada_w"][0], UC)
            w_up = a["ffn_w_up"][0].rearrange("(k p) (c u n) -> c u p k n", p=P, c=2, n=UC)
            w_down = a["ffn_w_down"][0].rearrange("(u k p) n -> u p k n", p=P, k=2)
            w_gin = cols(a["gdn_w_in_2"][0][:, 0:UC * (U_GOUT - U_GIN)], UC)
            w_gout = a["gdn_w_out_2"][0].rearrange("(u k p) n -> u p k n", p=P, k=2)
            w_lin = cols(a["gla_w_in_2"][0][:, 0:UC * (U_LOUT - U_LIN)], UC)
            w_lout = a["gla_w_out_2"][0].rearrange("(u k p) n -> u p k n", p=P, k=2)

            sp.dma_start(rows[0:KD, 0, :], a["c"][0].rearrange("(k n) -> k n", n=P)).then_inc(S("c_in"), 16)
            sp.dma_start(ident[:], a["consts"][:, 0:P]).then_inc(S("ident_in"), 16)
            sp.dma_start(ada_rows[0:ADA, :], a["ada_b"][0].rearrange("(u n) -> u n", n=UC)).then_inc(S("c_in"), 16)
            for s in range(4):
                sp.dma_start(ada[:, s], ada_v[s]).then_inc(ada_full[s], 16)
            for tt in range(TT):
                sp.dma_start(xres[:, tt, :], a["x"][0, tt * P:(tt + 1) * P, :]).then_inc(S("x_in"), 16)
            with sp.Fori(1, 5) as i:
                for s in range(4):
                    sp.wait_ge(S("ada_used"), i * 4 + s - 3)
                    sp.dma_start(ada[:, s], one(ada_v, i * 4 + s)).then_inc(ada_full[s], 16)
            unit(0, (0, w_up[0, 0]))
            unit(1, (1, w_up[1, 0]))
            for s in range(4):
                sp.wait_ge(S("ada_used"), ADA - 7 + s)
                sp.dma_start(ada[:, s], ada_v[ADA - 4 + s]).then_inc(ada_full[s], 16)
            with sp.Fori(1, UP // 2) as i:
                for s in range(2):
                    sp.wait_ge(unit_split, i * 2 + s - 1)
                    unit(None, (s, one(w_up[s], i)))

            def stream(first, n, view):
                with sp.Fori(0, n // 2) as i:
                    for s in range(2):
                        sp.wait_ge(unit_split, first + i * 2 + s - 1)
                        unit(None, ((first + s) % 2, one(view, i * 2 + s)))
                if n % 2:
                    sp.wait_ge(unit_split, first + n - 2)
                    unit(None, ((first + n - 1) % 2, view[n - 1]))

            stream(U_DOWN, DOWN, w_down)
            stream(U_GIN, U_GOUT - U_GIN, w_gin)
            stream(U_GOUT, GOUT, w_gout)
            stream(U_LIN, U_LOUT - U_LIN, w_lin)
            stream(U_LOUT, LOUT, w_lout)

            for tt in range(TT):
                sp.wait_ge(S("ln2_done"), tt + 1)
                sp.dma_start(out[0, tt * P:(tt + 1) * P, :], xres[:, tt, :]).then_inc(S("out_written"), 16)
            sp.wait_ge(S("out_written"), 16 * TT)

        @block.gpsimd
        def _(pool):
            nc.gpsimd.memset(ones[:], 1.0).then_inc(S("prepared"), 1)

            def low(u, s):
                pool.wait_ge(hi_done, u + 1)
                nc.gpsimd.tensor_tensor(wl[:, s, :], raw[:, s, :], wh[:, s, :].bitcast(f32), ALU.subtract)\
                    .then_inc(unit_split, 1)

            for tt in range(TT):
                pool.wait_ge(S("scaled"), tt + 1)
                pool.wait_ge(S("mods_done"), 1)
                nc.gpsimd.tensor_tensor(u_pool[:, tt, :], u_pool[:, tt, :], mods[:, 0, :], ALU.add).then_inc(S("u_ready"), 1)
            pool.wait_ge(S("pool_in"), 64)
            nc.gpsimd.tensor_tensor(pool_w[:], pool_w[:],
                                    gains[:, PSCALE, :].rearrange("p (g n) -> p g n", n=GDIM).unsqueeze(2)
                                    .broadcast_to([P, POOL_GROUPS, GDIM // P, GDIM]), ALU.mult).then_inc(S("prepared"), 1)
            low(0, 0)
            low(1, 1)
            for tt in range(TT):
                pool.wait_ge(S("scaled"), TT + NORM_ORDER.index(("u", tt)) + 1)
                nc.gpsimd.tensor_tensor(u_ffn[:, tt, :], u_ffn[:, tt, :], mods[:, 3, :], ALU.add).then_inc(S("u2_ready"), 1)
            with pool.Fori(1, (U_GIN + 1) // 2) as i:
                for s in range(2):
                    low(i * 2 + s, s)
            first = (U_GIN + 1) // 2 * 2
            last = U_GOUT + 2
            with pool.Fori(0, (last - first) // 2) as i:
                for s in range(2):
                    low(first + i * 2 + s, s)
            assert (last - first) % 2 == 1

            pool.wait_ge(S("factors"), 8)
            with pool.Fori(0, TT) as i:
                pool.wait_ge(S("vn_mm"), i * H + 1)
                pool.wait_ge(w_used, U_GOUT)
                nc.gpsimd.tensor_copy(k_now[:], qkt[:, 1, :, ds(i * P, P)]).then_inc(S("staged"), 1)
                pool.wait_ge(S("o_inv"), i * 4 + 1)
                pool.wait_ge(w_used, U_GOUT)
                nc.gpsimd.tensor_copy(scal_now[:], scal[:, :, ds(i, 1), :].rearrange("p n a h -> p n (a h)")).then_inc(S("staged"), 1)
                for l in range(LEVELS):
                    for g in range(2):
                        hs = slice(4 * g, 4 * g + 4)
                        if l == 0:
                            pool.wait_ge(S("u_done"), i * 2 + g + 1)
                        elif l == 1:
                            pool.wait_ge(S("y0_done"), i * 2 + g + 1)
                        else:
                            pool.wait_ge(S("p1_mm"), i * 12 + 2 * (l - 2) + g + 1)
                        nc.gpsimd.tensor_tensor(upper_m[:, hs, :], upper[:, hs, :],
                                                masks[:, l, :].unsqueeze(1).broadcast_to([P, 4, P]), ALU.mult)\
                            .then_inc(S("um_done"), 1)
                    if l in (1, 2):
                        g = l - 1
                        hs = slice(4 * g, 4 * g + 4)
                        nc.gpsimd.tensor_tensor(part[:, hs, :], part[:, hs, :],
                                                tri[:].unsqueeze(1).broadcast_to([P, 4, P]), ALU.mult)\
                            .then_inc(S("dec_done"), 1)
                        pool.wait_ge(S("dec_done"), i * 2 + g + 1)
                        pool.wait_ge(S("attn_raw"), i * 2 + g + 1)
                        nc.gpsimd.tensor_tensor(attn[:, hs, :], attn[:, hs, :], part[:, hs, :], ALU.mult)\
                            .then_inc(S("attn_done"), 1)

            low(last - 1, (last - 1) % 2)
            with pool.Fori(0, (U_LIN + 1 - last) // 2) as i:
                for s in range(2):
                    low(last + i * 2 + s, (last + s) % 2)
            at_u = last + (U_LIN + 1 - last) // 2 * 2
            with pool.Fori(0, (UNITS - at_u) // 2) as i:
                for s in range(2):
                    low(at_u + i * 2 + s, (at_u + s) % 2)
            if (UNITS - at_u) % 2:
                low(UNITS - 1, (UNITS - 1) % 2)
        @block.scalar
        def _(act):
            def high(u, s, nth):
                act.wait_ge(raw_full[s], (nth + 1) * 16)
                if not (isinstance(u, int) and u < 2):
                    act.wait_ge(w_used, u - 1)
                nc.scalar.activation(wh[:, s, :], raw[:, s, :], ACT.Copy).then_inc(hi_done, 1)

            def high_at(first, i, s):
                high(first + s + i * 2, (first + s) % 2, i + (first + s) // 2)

            sums = [0]

            def scratch_free():
                if sums[0]:
                    act.wait_ge(S("squares_summed"), sums[0])
                sums[0] += 1

            def square_sum(scratch, x, total):
                scratch_free()
                nc.scalar.activation(scratch, x, ACT.Square, accum_out=total).then_inc(S("squares_summed"), 1)

            roots = [0]

            def root(x):
                roots[0] += 1
                act.wait_ge(S("mean_done"), roots[0])
                nc.scalar.activation(x, x, ACT.Sqrt).then_inc(S("root_done"), 1)

            def parts_high(stage, tt, b):
                act.wait_ge(S("turned"), stage * TT + tt + 1)
                nc.scalar.activation(xth[:, :, tt * P:(tt + 1) * P],
                                     bank2(b).rearrange("p (k n) -> p k n", n=P), ACT.Copy).then_inc(S("parts_hi"), 1)

            def layer_norm_sums(first):
                for tt in range(TT + 1):
                    if tt < TT:
                        act.wait_ge(S("ln_sum"), first + tt + 1)
                        scratch_free()
                        nc.scalar.activation(junk_ln[:], xres[:, tt, :], ACT.Copy, accum_out=mv[:, tt, 0:1])\
                            .then_inc(S("squares_summed"), 1)
                    if tt >= 1:
                        root(mv[:, tt - 1, 1:2])
                    if tt < TT:
                        act.wait_ge(S("ln_mean"), first + tt + 1)
                        scratch_free()
                        nc.scalar.activation(junk_ln[:], xres[:, tt, :], ACT.Square, bias=mv[:, tt, 0:1], accum_out=mv[:, tt, 1:2])\
                            .then_inc(S("squares_summed"), 1)

            def row(dst, src, name):
                act.dma_start(dst, src.partition_broadcast(P)).then_inc(S(name), 16)

            act.dma_start(rows[KD:KD + LH, 0, :], a["gla_b_gk_2"][0].rearrange("(k n) -> k n", n=P)).then_inc(S("rows_in"), 16)
            cw = a["ffn_conv_w"][0].rearrange("j (k n) -> (j k) n", n=P)
            cb = a["ffn_conv_b"][0].rearrange("(k n) -> k n", n=P)
            nch = 2 * FC
            act.dma_start(rows[0:2 * nch, 1, :], cw[0:2 * nch, :]).then_inc(S("rows_in"), 16)
            act.dma_start(rows[0:nch, 2, :], cw[2 * nch:3 * nch, :]).then_inc(S("rows_in"), 16)
            act.dma_start(rows[nch:2 * nch, 2, :], cb).then_inc(S("rows_in"), 16)
            act.dma_start(rows[:, 3, :], a["gdn_conv_w_2"][0].rearrange("j (k n) -> (j k) n", n=P)).then_inc(S("rows_in"), 16)
            row(gains[:, PRE1, :], a["mix_pre_g"][0], "gains_in")

            act.wait_ge(S("rows_turned"), 1)
            nc.scalar.activation(c_col[:], ps[:, 6, 0:KD], ACT.Silu).then_inc(S("c_silu"), 1)
            for tt in range(TT):
                act.wait_ge(S("x_in"), 16 * TT)
                square_sum(junk[:], xres[:, tt, :], stat[:, 0, tt:tt + 1])
            root(stat[:, 0, 0:TT])
            act.dma_start(pool_band[:].rearrange("p g t n -> p (g t n)"), a["pool_band"]).then_inc(S("pool_in"), 16)
            act.dma_start(pool_w[:], a["pool_w"][0].rearrange("g (k p) n -> p g k n", p=P)).then_inc(S("pool_in"), 16)
            row(gains[:, PSCALE, :], a["pool_scale"][0], "pool_in")
            row(gains[:, POST1, :], a["mix_post_g"][0], "pool_in")
            for cb in range(KD):
                act.wait_ge(S("pool_mm"), cb + 1)
                nc.scalar.activation(pooled[:, cb, :], ps[:, 4 + cb % 4, :], ACT.Copy).then_inc(S("pooled_done"), 1)
            row(gains[:, PRE2, :], a["ffn_pre_g"][0], "late_gains_in")
            row(gains[:, POST2, :], a["ffn_post_g"][0], "late_gains_in")
            act.dma_start(tri[:], a["consts"][:, P:2 * P]).then_inc(S("masks_in"), 16)
            act.dma_start(masks[:].rearrange("p l n -> p (l n)"), a["consts"][:, 2 * P:]).then_inc(S("masks_in"), 16)
            act.dma_start(ba_raw[:], a["gdn_w_in_2"][0][:, UC * (U_GOUT - U_GIN):].rearrange("(k p) n -> p k n", p=P))\
                .then_inc(S("masks_in"), 16)
            for n, (what, tt) in enumerate(NORM_ORDER):
                if n == 2:
                    high(0, 0, 0)
                    high(1, 1, 0)
                if what == "y":
                    act.wait_ge(S("y_mm"), tt + 1)
                    square_sum(junk[:], bank2(4 + 2 * (tt % 2)), stat[:, 1, tt:tt + 1])
                    root(stat[:, 1, tt:tt + 1])
                else:
                    act.wait_ge(S("x1_done"), tt + 1)
                    square_sum(junk[:], xres[:, tt, :], stat[:, 2, tt:tt + 1])
                    root(stat[:, 2, tt:tt + 1])
            for tt in range(TT):
                parts_high(0, tt, 4 + 2 * (tt % 2))

            with act.Fori(0, UP // 2) as i:
                for s in range(2):
                    high_at(U_UP + 2, i, s)
                    for sub in range(2):
                        chunk = i * 2 + sub + s * FC
                        if sub == 0:
                            act.wait_ge(S("up_half"), i * 2 + s + 1)
                        else:
                            act.wait_ge(w_used, i * 2 + s + 1)
                        act.wait_ge(S("act_done"), i * 2 + sub + 1)
                        act.wait_ge(S("cols_done"), 3)
                        nc.scalar.activation(conv_out[:, s, sub, :], ps[:, 2 * s + sub, :], ACT.Identity,
                                             scale=conv_taps[:, 0, ds(chunk + 2 * FC, 1)],
                                             bias=conv_taps[:, 1, ds(chunk + 2 * FC, 1)]).then_inc(S("conv_mid"), 1)
                    if s == 0:
                        for sub in range(2):
                            act.wait_ge(S("conv_done"), i * 4 + sub + 5)
                            nc.scalar.activation(conv_out[:, 0, sub, :], conv_out[:, 0, sub, :], ACT.Gelu_apprx_tanh)\
                                .then_inc(S("gelu_done"), 1)
            with act.Fori(0, DOWN // 2) as i:
                for s in range(2):
                    high_at(U_DOWN + 2, i, s)
            for tt in range(TT):
                act.wait_ge(S("proj_mm"), tt + 1)
                square_sum(junk[:], bank2(2 * tt), stat[:, 3, tt:tt + 1])
                root(stat[:, 3, tt:tt + 1])
            for tt in range(TT):
                parts_high(1, tt, 2 * tt)
            high(U_DOWN + DOWN + 1, (U_DOWN + DOWN + 1) % 2, (U_DOWN + DOWN + 1) // 2)
            act.wait_ge(S("x2_done"), TT)
            row(norm_w[:], a["gdn_norm_w_2"][0], "alog_in")
            row(alog_dt[:, 0, :], a["gdn_a_log_2"][0], "alog_in")
            row(alog_dt[:, 1, :], a["gdn_dt_bias_2"][0], "alog_in")

            def conv_first(i, s, base, free):
                for sub in range(2):
                    if sub == 0:
                        act.wait_ge(S("qkv_half"), base + i * 2 + s + 1)
                    else:
                        act.wait_ge(w_used, U_GIN + base + i * 2 + s + 1)
                    free(i, s, sub)
                    act.wait_ge(S("cols_done"), 3)
                    nc.scalar.activation(conv_v[:, sub, :], ps[:, 2 * s + sub, :], ACT.Copy,
                                         scale=gdn_taps[:, 3, ds(base * 2 + i * 4 + 2 * s + sub, 1)]).then_inc(S("tap3"), 1)

            qk_flat = qkt[:].rearrange("p a h t -> p (a h) t")
            act.sem_inc(S("qk_silu"), 2)

            def squashed(i, s, sub):
                act.wait_ge(S("qk_silu"), i * 4 + 2 * s + sub + 1)
            with act.Fori(0, GIN_QK // 2) as i:
                for s in range(2):
                    high_at(U_GIN + 2, i, s)
                    conv_first(i, s, 0, squashed)
                    for sub in range(2):
                        act.wait_ge(S("qkv_conv"), i * 4 + 2 * s + sub + 5)
                        act.wait_ge(S("parts_lo"), 2 * TT)
                        nc.scalar.activation(qk_flat[:, ds(i * 4 + 2 * s + sub, 1), :].rearrange("p a t -> p (a t)"),
                                             conv_v[:, sub, :], ACT.Silu).then_inc(S("qk_silu"), 1)
            act.wait_ge(S("ba_mm"), 1)
            act.wait_ge(S("parts_lo"), 2 * TT)
            nc.scalar.activation(ba_cols[0:2 * H, :], ps[0:2 * H, 7, :], ACT.Copy).then_inc(S("ba_exp"), 1)
            act.wait_ge(S("ba_ready"), 1)
            nc.scalar.activation(ba_tmp[:, 0], ba_tmp[:, 0], ACT.Exp, scale=-1.0).then_inc(S("ba_exp"), 1)
            nc.scalar.activation(ba_tmp[:, 2], ba_tmp[:, 2], ACT.Exp).then_inc(S("ba_exp"), 1)
            act.wait_ge(S("ba_exp"), 3)
            nc.scalar.activation(ba_tmp[:, 2], ba_tmp[:, 2], ACT.Ln, bias=1.0).then_inc(S("ba_exp"), 1)
            act.wait_ge(S("alog_in"), 48)
            nc.scalar.activation(alog_dt[:, 0, :], alog_dt[:, 0, :], ACT.Exp).then_inc(S("ba_exp"), 1)
            act.wait_ge(S("qk_silu"), 2 + 2 * GIN_QK)
            with act.Fori(0, GIN_V // 2) as i:
                for s in range(2):
                    high_at(U_GIN + GIN_QK + 2, i, s)

                    def turned(i, s, sub):
                        act.wait_ge(S("v_turned"), i * 2 + s + 1)
                    conv_first(i, s, GIN_QK, turned)
                    for sub in range(2):
                        act.wait_ge(S("qkv_conv"), 2 * GIN_QK + i * 4 + 2 * s + sub + 5)
                        nc.scalar.activation(conv_v[:, sub, :], conv_v[:, sub, :], ACT.Silu).then_inc(S("v_silu"), 1)
            act.wait_ge(S("gc_ready"), 1)
            nc.scalar.activation(scal[:, KEG], scal[:, GC], ACT.Exp).then_inc(S("gc_exp"), 1)
            nc.scalar.activation(scal[:, KDS], scal[:, KDS], ACT.Exp).then_inc(S("gc_exp"), 1)
            nc.scalar.activation(scal[:, GL], ps[:, 7, 96:128].rearrange("p (t h) -> p t h", h=H), ACT.Exp).then_inc(S("gc_exp"), 1)
            root(scal[:, RKI].rearrange("p t h -> p (t h)"))
            root(scal[:, QS].rearrange("p t h -> p (t h)"))
            gate_flat = gate[:].rearrange("p t h v -> p t (h v)")
            with act.Fori(0, GIN_GATE // 2) as i:
                for s in range(2):
                    act.wait_ge(w_used, U_GIN + GIN_QK + GIN_V + i * 2 + s + 1)
                    act.wait_ge(S("parts_lo"), 2 * TT)
                    nc.scalar.activation(gate_flat[:, :, ds((i * 2 + s) * UC, UC)],
                                         bank2(2 * s).rearrange("p (t n) -> p t n", n=UC), ACT.Silu).then_inc(S("gate_silu"), 1)
                    high_at(U_GIN + GIN_QK + GIN_V + 2, i, s)

            with act.Fori(0, TT) as i:
                for g in range(2):
                    hs = slice(4 * g, 4 * g + 4)
                    act.wait_ge(S("dec_diff"), i * 2 + g + 1)
                    nc.scalar.activation(part[:, hs, :], part[:, hs, :], ACT.Exp).then_inc(S("dec_exp"), 1)
                    nc.scalar.activation(prod[:, hs, :], heads4(2 * g), ACT.Exp).then_inc(S("eg_done"), 1)
                for g in range(2):
                    act.wait_ge(S("u_done"), i * 2 + g + 1)
                    for h in range(4 * g, 4 * g + 4):
                        b, o = (1, 3, 4, 5)[h // 2], (h % 2) * 2 * P
                        sc = nc.scalar.activation(attn[:, h, :], ps[:, b, o:o + P], ACT.Copy, scale=scal_now[:, RK, h:h + 1])
                    sc.then_inc(S("attn_raw"), 1)
                for g in range(2):
                    hs = slice(4 * g, 4 * g + 4)
                    act.wait_ge(S("x0_mm"), i * 2 + g + 1)
                    nc.scalar.activation(tri_inv_t[:, hs, :], ps[:, 2 * g, :].rearrange("p (h n) -> p h n", n=P), ACT.Copy)\
                        .then_inc(S("x0_done"), 1)
                for l in range(1, LEVELS):
                    for g in range(2):
                        hs = slice(4 * g, 4 * g + 4)
                        act.wait_ge(S("p1_mm"), i * 12 + 2 * (l - 1) + g + 1)
                        act.wait_ge(S("qdec_done"), i * 2 + g + 1)
                        nc.scalar.activation(prod[:, hs, :], heads4(2 * g), ACT.Copy)\
                            .then_inc(S("p1_done"), 1)
                for g in range(2):
                    act.wait_ge(S("um_done"), i * 14 + 13 + g)
                    act.wait_ge(S("ktok_mm"), i + 1)
                    for h in range(4 * g, 4 * g + 4):
                        ke = nc.scalar.activation(k_in[:, h, :], ps[:, 6 + g, (h % 4) * P:(h % 4 + 1) * P], ACT.Copy,
                                                  scale=scal_now[:, KEG, h:h + 1])
                    ke.then_inc(S("kin_done"), 1)
                for g in range(2):
                    hs = slice(4 * g, 4 * g + 4)
                    act.wait_ge(S("w_mm"), i * 2 + g + 1)
                    act.wait_ge(S("attn_done"), i * 2 + g + 1)
                    nc.scalar.activation(part[:, hs, :], ps[:, 2 * g, :].rearrange("p (h n) -> p h n", n=P), ACT.Copy, scale=-1.0)\
                        .then_inc(S("w_done"), 1)
                for g in range(2):
                    for h in range(4 * g, 4 * g + 4):
                        act.wait_ge(S("o_mm"), i * H + (h | 1) + 1)
                        sq = nc.scalar.activation(gated_now[:, h, :], ps[:, (0, 2, 6, 7)[h // 2], (h % 2) * DV:(h % 2 + 1) * DV],
                                                  ACT.Square, accum_out=coef[:, 0, h:h + 1])
                    sq.then_inc(S("o_ss"), 1)
                    hs = slice(4 * g, 4 * g + 4)
                    act.wait_ge(S("o_ms"), i * 2 + g + 1)
                    nc.scalar.activation(coef[:, 1, hs], coef[:, 1, hs], ACT.Sqrt).then_inc(S("o_rt"), 1)
                for b in range(4):
                    act.wait_ge(S("og_turned"), i * 4 + b + 1)
                    act.wait_ge(S("gate_done"), GIN_GATE)
                    nc.scalar.activation(ogt_h[:, ds(i, 1), 4 * b:4 * b + 4, :].rearrange("p a k n -> p (a k) n"),
                                         ps[:, (1, 3, 4, 5)[b], :].rearrange("p (k n) -> p k n", n=P), ACT.Copy)\
                        .then_inc(S("ogt_hi"), 1)
            act.wait_ge(S("s_done"), TT * H)
            row(ln_gb[:, 0, :], a["ln_g_2"][0], "ln1_in")
            row(ln_gb[:, 1, :], a["ln_b_2"][0], "ln1_in")
            with act.Fori(0, GOUT // 2 - 1) as i:
                for s in range(2):
                    high_at(U_GOUT + 2, i, s)
            high_at(U_GOUT + 2, GOUT // 2 - 1, 0)
            layer_norm_sums(0)
            act.wait_ge(w_used, U_LIN)
            act.dma_start(low_raw[:], a["gla_w_in_2"][0][:, UC * (U_LOUT - U_LIN):].rearrange("(k p) n -> p k n", p=P))\
                .then_inc(S("low_in"), 16)
            act.dma_start(gk_up[0:16, :], a["gla_w_gk_up_2"][0]).then_inc(S("low_in"), 16)
            row(norm_w2[:], a["gla_norm_w_2"][0], "low_in")
            for tt in range(TT):
                parts_high(2, tt, 2 * tt)
            high_at(U_GOUT + 2, GOUT // 2 - 1, 1)
            act.wait_ge(S("ln1_done"), TT)
            row(ln_gb[:, 0, :], a["ln_g_2"][1], "ln2_in")
            row(ln_gb[:, 1, :], a["ln_b_2"][1], "ln2_in")

            act.wait_ge(S("low_mm"), 1)
            nc.scalar.activation(gk_low[0:16, :], ps[0:16, 0, :], ACT.Copy).then_inc(S("gk_low_done"), 1)

            def qk_unit(j):
                u = U_LIN + j
                high(u + 2, u % 2, (u + 2) // 2)
                act.wait_ge(w_used, u + 1)
                dst = (qg if j < LIN_QK // 2 else kg)[:, 2 * (j % 2):2 * (j % 2) + 2, :]
                nc.scalar.activation(dst, ps[:, 2 * (j % 2):2 * (j % 2) + 2, :], ACT.Copy,
                                     scale=KEY_SCALE if j < LIN_QK // 2 else 1.0).then_inc(S("lqk_done"), 1)
            qk_unit(0)
            for h in range(LH):
                act.wait_ge(S("gk_mm"), h + 1)
                nc.scalar.activation(zg[:, h, :], ps[:, 4 + h, :], ACT.Identity, bias=bgk_col[:, h:h + 1]).then_inc(S("gk_z"), 1)
            act.wait_ge(S("gk_abs"), 1)
            nc.scalar.activation(eg[:], eg[:], ACT.Exp).then_inc(S("gk_exp"), 1)
            act.wait_ge(S("gk_exp"), 1)
            nc.scalar.activation(eg[:], eg[:], ACT.Ln, bias=1.0).then_inc(S("gk_exp"), 1)
            for j in range(1, LIN_QK):
                qk_unit(j)
            act.wait_ge(S("kd_diff"), 1)
            nc.scalar.activation(eg[:], eg[:], ACT.Exp, scale=1.0 / GATE_NORM).then_inc(S("kd_exp"), 1)
            nc.scalar.activation(glast_exp[:], bg[:].rearrange("p h (t c) -> p h t c", c=P)[:, :, :, P - 1], ACT.Exp,
                                 scale=1.0 / GATE_NORM).then_inc(S("kd_exp"), 1)
            for j in range(LIN_V + LIN_GATE):
                u = U_LIN + LIN_QK + j
                if j >= 1:
                    act.wait_ge(S("lev_diff"), j)
                    nc.scalar.activation(eg[:], eg[:], ACT.Exp, scale=1.0 / GATE_NORM).then_inc(S("lev_exp"), 1)
                if j == 1:
                    act.wait_ge(S("kd_turned"), LH)
                    for h in range(LH):
                        nc.scalar.activation(kd_tok[:, h], ps[:, 4 + h, :].rearrange("p (t n) -> p t n", n=P), ACT.Copy)\
                            .then_inc(S("kd_done"), 1)
                high(u + 2, u % 2, (u + 2) // 2)
                act.wait_ge(w_used, u + 1)
                src = bank2(2 * (j % 2)).rearrange("p (t n) -> p t n", n=UC)
                if j < LIN_V:
                    nc.scalar.activation(vg[:, :, j, :], src, ACT.Copy).then_inc(S("lv_done"), 1)
                else:
                    nc.scalar.activation(gg[:, :, j - LIN_V, :], src, ACT.Silu).then_inc(S("lv_done"), 1)
            act.wait_ge(S("lev_z"), LEVELS)
            nc.scalar.activation(eg[:], bg[:], ACT.Exp, scale=1.0 / GATE_NORM).then_inc(S("qe_exp"), 1)
            for tt in range(TT):
                for h in range(LH):
                    act.wait_ge(S("lo_mm"), tt * LH + (h | 1) + 1)
                    square_sum(junk_g[:], ps[:, O_BANK[tt] + h // 2, (h % 2) * DV:(h % 2 + 1) * DV], stat[:, 4 + tt, h:h + 1])
                root(stat[:, 4 + tt, 0:LH])
            for tt in range(TT):
                parts_high(3, tt, O_BANK[tt])
            for j in range(2, LOUT):
                high(U_LOUT + j, (U_LOUT + j) % 2, (U_LOUT + j) // 2)
            layer_norm_sums(TT)
        @block.vector
        def _(v):
            V = nc.vector

            seen = {}

            def own(name):
                seen[name] = seen.get(name, 0) + 1
                v.wait_ge(S(name), seen[name])

            roots = [0]

            def inv_root(x, total, eps, count):
                v.wait_ge(S("squares_summed"), count)
                V.tensor_scalar(x, x, 1.0 / total, eps, ALU.mult, ALU.add).then_inc(S("mean_done"), 1)
                inverse(x)

            def inverse(x):
                roots[0] += 1
                v.wait_ge(S("root_done"), roots[0])
                V.reciprocal(x, x).then_inc(S("inverse_done"), 1)
                own("inverse_done")

            def parts_low(stage, tt, b):
                v.wait_ge(S("parts_hi"), stage * TT + tt + 1)
                cols = slice(tt * P, (tt + 1) * P)
                V.tensor_tensor(xtl[:, :, cols], bank2(b).rearrange("p (k n) -> p k n", n=P),
                                xth[:, :, cols].bitcast(f32), ALU.subtract).then_inc(S("parts_lo"), 1)

            v.wait_ge(S("rows_turned"), 1)
            v.wait_ge(S("c_silu"), 1)
            V.tensor_copy(bgk_col[:], ps[:, 6, KD:KD + LH]).then_inc(S("cols_done"), 1)
            V.tensor_copy(conv_taps[:].rearrange("p a n -> p (a n)"), ps[:, 7, 16:16 + 8 * FC]).then_inc(S("cols_done"), 1)
            V.tensor_copy(gdn_taps[:].rearrange("p a n -> p (a n)"), ps[:, 7, 16 + 8 * FC:16 + 8 * FC + P]).then_inc(S("cols_done"), 1)

            def partials(j, which=(0, 1)):
                for m in which:
                    v.wait_ge(ada_full[2 * m + 1], 16 * (j + 1))
                    if j >= 2:
                        v.wait_ge(S("ada_used"), 4 * (j - 1))
                    for k in range(KD):
                        w, acc = ada[:, 2 * m + 1, k, :], partial[:, j % 2, m, :]
                        if k == 0:
                            V.tensor_scalar(acc, w, c_col[:, 0:1], None, ALU.mult).then_inc(S("partials"), 1)
                        else:
                            own("partials")
                            V.scalar_tensor_tensor(acc, w, c_col[:, k:k + 1], acc, ALU.mult, ALU.add).then_inc(S("partials"), 1)
                    own("partials")

            def mod(j):
                v.wait_ge(S("ada_used"), 4 * (j + 1))
                src = bank2(2 * (j % 2))
                if j in (0, 3):
                    V.tensor_copy(mods[:, j, :], src).then_inc(S("mods_done"), 1)
                elif j in (1, 4):
                    v.wait_ge(S("gains_in"), 16)
                    if j == 4:
                        v.wait_ge(S("late_gains_in"), 32)
                    V.scalar_tensor_tensor(mods[:, j, :], src, 1.0, gains[:, PRE1 if j == 1 else PRE2, :],
                                           ALU.add, ALU.mult).then_inc(S("mods_done"), 1)
                else:
                    if j == 2:
                        v.wait_ge(S("pool_in"), 64)
                    else:
                        v.wait_ge(S("late_gains_in"), 32)
                    V.tensor_tensor(mods[:, j, :], src, gains[:, POST1 if j == 2 else POST2, :], ALU.mult).then_inc(S("mods_done"), 1)

            def norm(what, tt):
                count = TT + NORM_ORDER.index((what, tt)) + 1
                if what == "y":
                    inv_root(stat[:, 1, tt:tt + 1], D, EPS, count)
                    v.wait_ge(S("mods_done"), 3)
                    V.scalar_tensor_tensor(y_pool[:, tt, :], bank2(4 + 2 * (tt % 2)), stat[:, 1, tt:tt + 1], mods[:, 2, :],
                                           ALU.mult, ALU.mult).then_inc(S("scaled"), 1)
                    own("scaled")
                    V.tensor_tensor(xres[:, tt, :], xres[:, tt, :], y_pool[:, tt, :], ALU.add).then_inc(S("x1_done"), 1)
                else:
                    inv_root(stat[:, 2, tt:tt + 1], D, EPS, count)
                    v.wait_ge(S("mods_done"), 5)
                    v.wait_ge(S("y_mm"), TT)
                    V.scalar_tensor_tensor(u_ffn[:, tt, :], xres[:, tt, :], stat[:, 2, tt:tt + 1], mods[:, 4, :],
                                           ALU.mult, ALU.mult).then_inc(S("scaled"), 1)
                    seen["scaled"] += 1

            partials(0)
            inv_root(stat[:, 0, 0:TT], D, EPS, TT)
            partials(1)
            mod(0)
            mod(1)
            v.wait_ge(S("mods_done"), 2)
            for tt in range(TT):
                V.scalar_tensor_tensor(u_pool[:, tt, :], xres[:, tt, :], stat[:, 0, tt:tt + 1], mods[:, 1, :],
                                       ALU.mult, ALU.mult).then_inc(S("scaled"), 1)
                seen["scaled"] = tt + 1
            partials(2)
            mod(2)
            partials(3)
            mod(3)
            partials(4, [0])
            for what, tt in NORM_ORDER[:2]:
                norm(what, tt)
            partials(4, [1])
            mod(4)
            for what, tt in NORM_ORDER[2:]:
                norm(what, tt)
            for tt in range(TT):
                parts_low(0, tt, 4 + 2 * (tt % 2))
            mod(5)

            v.sem_inc(S("conv_done"), 4)
            v.sem_inc(S("act_done"), 2)
            def taps_and_product(i):
                for s in range(2):
                    for sub in range(2):
                        chunk = i * 2 + sub + s * FC
                        src, dst = ps[:, 2 * s + sub, :], conv_out[:, s, sub, :]
                        v.wait_ge(S("conv_mid"), i * 4 + 2 * s + sub + 1)
                        V.scalar_tensor_tensor(dst[:, 1:T], src[:, 0:T - 1], conv_taps[:, 0, ds(chunk, 1)], dst[:, 1:T],
                                               ALU.mult, ALU.add).then_inc(S("conv_left"), 1)
                        v.wait_ge(S("conv_left"), i * 4 + 2 * s + sub + 1)
                        V.scalar_tensor_tensor(dst[:, 0:T - 1], src[:, 1:T], conv_taps[:, 1, ds(chunk, 1)], dst[:, 0:T - 1],
                                               ALU.mult, ALU.add).then_inc(S("conv_done"), 1)
                        if s == 1:
                            v.wait_ge(S("conv_done"), i * 4 + 7 + sub)
                            v.wait_ge(S("gelu_done"), i * 2 + sub + 1)
                            V.tensor_tensor(acts[:, ds(i * 2 + sub, 1), :].rearrange("p a t -> p (a t)"),
                                            conv_out[:, 0, sub, :], conv_out[:, 1, sub, :], ALU.mult).then_inc(S("act_done"), 1)
            def act_parts(u):
                for kk in range(2):
                    k, slot = u * 2 + kk, (u % 2) * 2 + kk
                    if u >= 2:
                        v.wait_ge(w_used, U_DOWN + u - 1)
                    V.tensor_copy(act_parts_h[:, slot, :], acts[:, k, :]).then_inc(S("act_hi"), 1)
                    v.wait_ge(S("act_hi"), k + 1)
                    V.tensor_tensor(act_parts_l[:, slot, :], acts[:, k, :], act_parts_h[:, slot, :].bitcast(f32), ALU.subtract)\
                        .then_inc(S("act_split"), 1)

            with v.Fori(0, UP // 2 - 1) as i:
                taps_and_product(i)
            v.wait_ge(S("act_done"), 2 + 4)
            act_parts(0)
            act_parts(1)
            taps_and_product(UP // 2 - 1)
            v.wait_ge(S("act_done"), 2 + FC)
            for u in range(2, DOWN):
                act_parts(u)
            v.wait_ge(S("masks_in"), 48)
            V.tensor_copy(ba_h[:], ba_raw[:]).then_inc(S("ba_hi"), 1)
            v.wait_ge(S("ba_hi"), 1)
            V.tensor_tensor(ba_l[:], ba_raw[:], ba_h[:].bitcast(f32), ALU.subtract).then_inc(S("ba_split"), 1)
            for tt in range(TT):
                inv_root(stat[:, 3, tt:tt + 1], D, EPS, 3 * TT + tt + 1)
                V.scalar_tensor_tensor(f_scaled[:, tt, :], bank2(2 * tt), stat[:, 3, tt:tt + 1], mods[:, 5, :],
                                       ALU.mult, ALU.mult).then_inc(S("scaled"), 1)
                own("scaled")
                V.tensor_tensor(xres[:, tt, :], xres[:, tt, :], f_scaled[:, tt, :], ALU.add).then_inc(S("x2_done"), 1)
            for tt in range(TT):
                parts_low(1, tt, 2 * tt)

            def th(x):
                return x.rearrange("p (t h) -> p t h", h=H)

            def taps(n, s, sub):
                src, dst = ps[:, 2 * s + sub, :], conv_v[:, sub, :]
                v.wait_ge(S("tap3"), n + 1)
                for j in (1, 2, 3):
                    w = gdn_taps[:, 3 - j, ds(n, 1)] if not isinstance(n, int) else gdn_taps[:, 3 - j, n:n + 1]
                    if j > 1:
                        v.wait_ge(S("tap_mid"), n * 2 + j - 1)
                    V.scalar_tensor_tensor(dst[:, j:T], src[:, 0:T - j], w, dst[:, j:T], ALU.mult, ALU.add)\
                        .then_inc(S("qkv_conv") if j == 3 else S("tap_mid"), 1)

            def unit_taps(n, s):
                for sub in range(2):
                    taps(n * 2 + sub, s, sub)

            def values(h):
                v.wait_ge(S("v_turned"), h + 2)
                v.wait_ge(S("parts_lo"), 2 * TT)
                dst = val[:, :, h, :] if isinstance(h, int) else val[:, :, ds(h, 1), :].rearrange("p t a n -> p t (a n)")
                V.tensor_copy(dst, bank2(4).rearrange("p (t n) -> p t n", n=DV)).then_inc(S("val_done"), 1)

            qk_flat = qkt[:].rearrange("p a h t -> p (a h) t")

            def square(n, s):
                v.wait_ge(S("ss_mm"), n + 1)
                v.wait_ge(S("qk_silu"), n * 2 + 4)
                x = qk_flat[:, ds(n * 2, 2), :]
                V.tensor_tensor(squares[:, s], x, x, ALU.mult).then_inc(S("sq_done"), 1)

            v.sem_inc(S("qkv_conv"), 4)
            unit_taps(0, 0)
            square(0, 0)
            unit_taps(1, 1)
            square(1, 1)
            with v.Fori(1, GIN_QK // 2) as i:
                for s in range(2):
                    unit_taps(i * 2 + s, s)
                    square(i * 2 + s, s)
            ba = ps[:, 6, 2 * H * TT:4 * H * TT].rearrange("p (t n) -> p t n", n=2 * H)
            v.wait_ge(S("ba_turned"), 1)
            v.wait_ge(S("alog_in"), 48)
            V.tensor_tensor(ba_tmp[:, 1], ba[:, :, H:2 * H], alog_dt[:, 1, :].unsqueeze(1).broadcast_to([P, TT, H]), ALU.add)\
                .then_inc(S("ba_z"), 1)
            V.tensor_copy(ba_tmp[:, 0], ba[:, :, 0:H]).then_inc(S("ba_z"), 1)
            v.wait_ge(S("ba_z"), 2)
            V.scalar_tensor_tensor(ba_tmp[:, 2], ba_tmp[:, 1], -1.0, ba_tmp[:, 1], ALU.mult, ALU.min).then_inc(S("ba_ready"), 1)
            v.wait_ge(S("ba_exp"), 5)
            V.tensor_scalar(ba_tmp[:, 0], ba_tmp[:, 0], 1.0, None, ALU.add).then_inc(S("ba_z"), 1)
            V.scalar_tensor_tensor(ba_tmp[:, 3], ba_tmp[:, 1], 0.0, ba_tmp[:, 2], ALU.max, ALU.add).then_inc(S("ba_z"), 1)
            v.wait_ge(S("ba_z"), 4)
            V.reciprocal(ba_tmp[:, 0], ba_tmp[:, 0]).then_inc(S("beta_done"), 1)
            V.scalar_tensor_tensor(scal[:, GLOG], ba_tmp[:, 3], -1.0, alog_dt[:, 0, :].unsqueeze(1).broadcast_to([P, TT, H]),
                                   ALU.mult, ALU.mult).then_inc(S("glog_done"), 1)
            unit_taps(GIN_QK, 0)
            with v.Fori(0, GIN_V // 2 - 1) as i:
                for s in range(2):
                    unit_taps(i * 2 + GIN_QK + 1 + s, 1 - s)
                    values(i * 2 + s)
            v.wait_ge(S("gc_mm"), 1)
            V.tensor_copy(scal[:, GC], th(ps[:, 7, 64:96])).then_inc(S("gc_copied"), 1)
            v.wait_ge(S("gc_copied"), 1)
            V.tensor_tensor(scal[:, KDS], th(ps[:, 7, 96:128]), scal[:, GC], ALU.subtract).then_inc(S("gc_ready"), 1)
            sums = ps[:, 6, 0:2 * H * TT].rearrange("p (a h t) -> p a t h", a=2, t=TT)
            v.wait_ge(S("ss_mm"), 2 + GIN_QK)
            V.tensor_scalar(scal[:, RKI], sums[:, 1], EPS, None, ALU.add).then_inc(S("mean_done"), 1)
            V.tensor_scalar(scal[:, QS], sums[:, 0], EPS, None, ALU.add).then_inc(S("mean_done"), 1)
            unit_taps(GIN_QK + GIN_V - 1, 1)
            values(GIN_V - 2)
            values(GIN_V - 1)
            count = [0]

            def step(ins):
                count[0] += 1
                ins.then_inc(S("factors"), 1)
                v.wait_ge(S("factors"), count[0])

            roots[0] += 2
            v.wait_ge(S("root_done"), roots[0])
            v.wait_ge(S("gc_exp"), 3)
            v.wait_ge(S("beta_done"), 1)
            step(V.reciprocal(scal[:, RK], scal[:, RKI]))
            step(V.reciprocal(scal[:, QA], scal[:, QS]))
            step(V.tensor_scalar(scal[:, QS], scal[:, QA], KEY_SCALE, None, ALU.mult))
            step(V.scalar_tensor_tensor(scal[:, QA], scal[:, QA], KEY_SCALE * KEY_SCALE / DV, scal[:, QA], ALU.mult, ALU.mult))
            step(V.tensor_tensor(scal[:, VSC], ba_tmp[:, 0], scal[:, RK], ALU.mult))
            step(V.tensor_tensor(scal[:, BSC], scal[:, VSC], scal[:, RK], ALU.mult))
            step(V.tensor_tensor(scal[:, KEG], scal[:, KEG], scal[:, RK], ALU.mult))
            step(V.tensor_tensor(scal[:, KDS], scal[:, KDS], scal[:, RK], ALU.mult))
            with v.Fori(0, GIN_GATE // 2) as i:
                for s in range(2):
                    v.wait_ge(S("gate_silu"), i * 2 + s + 1)
                    g = gate[:, :, ds(i * 2 + s, 1), :].rearrange("p t a n -> p t (a n)")
                    V.tensor_tensor(g, g, norm_w[:].unsqueeze(1).broadcast_to([P, TT, DV]), ALU.mult).then_inc(S("gate_done"), 1)

            v.sem_inc(S("o_inv"), 1)
            v.sem_inc(S("ogt_lo"), 1)
            v.wait_ge(S("gate_done"), GIN_GATE)
            V.memset(state[:], 0.0).then_inc(S("state_zero"), 1)
            with v.Fori(0, TT) as i:
                tok = ds(i * P, P)
                for g in range(2):
                    v.wait_ge(S("gcrow_mm"), i * 2 + g + 1)
                    for h in range(4 * g, 4 * g + 4):
                        dd = V.tensor_scalar(part[:, h, :], ps[:, 2 * g, (h % 4) * P:(h % 4 + 1) * P], scal_now[:, GC, h:h + 1], 0.0,
                                             ALU.subtract, ALU.min)
                    dd.then_inc(S("dec_diff"), 1)
                for g in range(2):
                    v.wait_ge(S("raw_mm"), i * 2 + g + 1)
                    v.wait_ge(S("dec_exp"), i * 2 + g + 1)
                    for h in range(4 * g, 4 * g + 4):
                        b, o = (1, 3, 4, 5)[h // 2], (h % 2) * 2 * P
                        uu = V.scalar_tensor_tensor(upper[:, h, :], ps[:, b, o + P:o + 2 * P], scal_now[:, BSC, h:h + 1],
                                                    part[:, h, :], ALU.mult, ALU.mult)
                    uu.then_inc(S("u_done"), 1)
                v.wait_ge(S("ktok_mm"), i + 1)
                for g in range(2):
                    hs = slice(4 * g, 4 * g + 4)
                    v.wait_ge(S("um_done"), i * 14 + g + 1)
                    V.tensor_tensor(tri_inv[:, hs, :], ident[:].unsqueeze(1).broadcast_to([P, 4, P]), upper_m[:, hs, :],
                                    ALU.subtract).then_inc(S("y0_done"), 1)
                    v.wait_ge(S("eg_done"), i * 2 + g + 1)
                    V.tensor_tensor(q_dec[:, hs, :], qkt[:, 0, hs, tok], prod[:, hs, :], ALU.mult).then_inc(S("qdec_done"), 1)
                for l in range(1, LEVELS):
                    for g in range(2):
                        hs = slice(4 * g, 4 * g + 4)
                        v.wait_ge(S("xy_mm"), i * 12 + 2 * (l - 1) + g + 1)
                        left_x, right_y = halves(tri_inv_t[:, hs, :], l, 0), halves(tri_inv[:, hs, :], l, 1)
                        if l < LEVELS - 1:
                            V.tensor_tensor(left_x, left_x, halves(heads4(2 * g + 1), l, 0), ALU.subtract)
                        V.tensor_tensor(right_y, right_y, halves(heads4(4 + g), l, 1), ALU.subtract).then_inc(S("xy_done"), 1)
                        if l == LEVELS - 1:
                            v.wait_ge(S("xy_done"), i * 12 + 2 * (l - 1) + g + 1)
                            for h in range(4 * g, 4 * g + 4):
                                yy = V.tensor_scalar(tri_inv[:, h, :], tri_inv[:, h, :], scal_now[:, RKI, h:h + 1], None, ALU.mult)
                            yy.then_inc(S("yfin_done"), 1)
                for g in range(2):
                    v.wait_ge(S("kin_done"), i * 2 + g + 1)
                    for h in range(4 * g, 4 * g + 4):
                        kd = V.tensor_scalar(k_dec[:, h, :], ps[:, 6 + g, (h % 4) * P:(h % 4 + 1) * P], scal_now[:, KDS, h:h + 1], None,
                                             ALU.mult)
                    kd.then_inc(S("kdec_done"), 1)
                for h in range(H):
                    v.wait_ge(S("vn_mm"), i * H + (h | 1) + 2)
                    V.tensor_scalar(val[:, ds(i, 1), h, :].rearrange("p a n -> p (a n)"),
                                    ps[:, (1, 3, 4, 5)[h // 2], (h % 2) * DV:(h % 2 + 1) * DV], scal_now[:, VSC, h:h + 1], None,
                                    ALU.mult).then_inc(S("vn_done"), 1)
                def new_state(heads):
                    for h in heads:
                        v.wait_ge(S("kv_mm"), i * H + (h | 1) + 1)
                        V.scalar_tensor_tensor(state[:, h, :], state[:, h, :], scal_now[:, GL, h:h + 1],
                                               ps[:, (1, 3, 4, 5)[h // 2], (h % 2) * DV:(h % 2 + 1) * DV], ALU.mult, ALU.add)\
                            .then_inc(S("s_done"), 1)

                def mean_square(g):
                    hs = slice(4 * g, 4 * g + 4)
                    v.wait_ge(S("o_ss"), i * 2 + g + 1)
                    V.tensor_tensor(coef[:, 1, hs], coef[:, 0, hs], scal_now[:, QA, hs], ALU.mult).then_inc(S("o_mean"), 1)
                    v.wait_ge(S("o_mean"), i * 2 + g + 1)
                    V.tensor_scalar(coef[:, 1, hs], coef[:, 1, hs], EPS, None, ALU.add).then_inc(S("o_ms"), 1)

                def gated(g):
                    hs = slice(4 * g, 4 * g + 4)
                    v.wait_ge(S("o_rt"), i * 2 + g + 1)
                    V.reciprocal(coef[:, 2, hs], coef[:, 1, hs]).then_inc(S("o_inv"), 1)
                    v.wait_ge(S("o_inv"), i * 4 + 2 * g + 2)
                    V.tensor_tensor(coef[:, 3, hs], coef[:, 2, hs], scal_now[:, QS, hs], ALU.mult).then_inc(S("o_inv"), 1)
                    v.wait_ge(S("o_inv"), i * 4 + 2 * g + 3)
                    for h in range(4 * g, 4 * g + 4):
                        V.scalar_tensor_tensor(gated_now[:, h, :], ps[:, (0, 2, 6, 7)[h // 2], (h % 2) * DV:(h % 2 + 1) * DV],
                                               coef[:, 3, h:h + 1], gate[:, ds(i, 1), h, :].rearrange("p a n -> p (a n)"),
                                               ALU.mult, ALU.mult).then_inc(S("og_done"), 1)

                new_state(range(4))
                mean_square(0)
                new_state(range(4, 6))
                gated(0)
                new_state(range(6, 8))
                mean_square(1)
                gated(1)
                for b in range(4):
                    v.wait_ge(S("ogt_hi"), i * 4 + b + 1)
                    V.tensor_tensor(ogt_l[:, ds(i, 1), 4 * b:4 * b + 4, :].rearrange("p a k n -> p (a k) n"),
                                    ps[:, (1, 3, 4, 5)[b], :].rearrange("p (k n) -> p k n", n=P),
                                    ogt_h[:, ds(i, 1), 4 * b:4 * b + 4, :].rearrange("p a k n -> p (a k) n").bitcast(f32),
                                    ALU.subtract).then_inc(S("ogt_lo"), 1)

            def layer_norm(stage, name, summed):
                v.wait_ge(S(name + "_in"), 32)
                for step in range(TT + 2):
                    if step < TT:
                        tt = step
                        v.wait_ge(S("proj_mm"), stage * TT + tt + 1)
                        V.scalar_tensor_tensor(xres[:, tt, :], xres[:, tt, :], ALPHA, bank2(2 * tt), ALU.mult, ALU.add)\
                            .then_inc(S("ln_sum"), 1)
                    if 1 <= step <= TT:
                        tt = step - 1
                        v.wait_ge(S("squares_summed"), summed + 2 * tt + 2)
                        V.tensor_scalar(mv[:, tt, 1:2], mv[:, tt, 1:2], 1.0 / D, LN_EPS, ALU.mult, ALU.add).then_inc(S("mean_done"), 1)
                        V.scalar_tensor_tensor(xres[:, tt, :], xres[:, tt, :], mv[:, tt, 0:1], ln_gb[:, 0, :],
                                               ALU.add, ALU.mult).then_inc(S("ln_norm"), 1)
                    if step < TT:
                        tt = step
                        v.wait_ge(S("squares_summed"), summed + 2 * tt + 1)
                        V.tensor_scalar(mv[:, tt, 0:1], mv[:, tt, 0:1], -1.0 / D, None, ALU.mult).then_inc(S("ln_mean"), 1)
                    if step >= 2:
                        tt = step - 2
                        inverse(mv[:, tt, 1:2])
                        own("ln_norm")
                        V.scalar_tensor_tensor(xres[:, tt, :], xres[:, tt, :], mv[:, tt, 1:2], ln_gb[:, 1, :],
                                               ALU.mult, ALU.add).then_inc(S(name + "_done"), 1)

            layer_norm(1, "ln1", 4 * TT)
            for tt in range(TT):
                parts_low(2, tt, 2 * tt)

            v.wait_ge(S("low_in"), 48)
            V.tensor_copy(low_h[:], low_raw[:]).then_inc(S("low_hi"), 1)
            v.wait_ge(S("low_hi"), 1)
            V.tensor_tensor(low_l[:], low_raw[:], low_h[:].bitcast(f32), ALU.subtract).then_inc(S("low_split"), 1)
            flat = "p h t -> p (h t)"
            V.memset(attn_g[:], 1.0).then_inc(S("reset_set"), 1)
            v.wait_ge(S("reset_set"), 1)
            V.memset(attn_g[:].rearrange("p h (t c) -> p h t c", c=P)[:, :, :, 0:1], 0.0).then_inc(S("reset_set"), 1)
            v.wait_ge(S("gk_z"), LH)
            V.scalar_tensor_tensor(eg[:], zg[:], -1.0, zg[:], ALU.mult, ALU.min).then_inc(S("gk_abs"), 1)
            v.wait_ge(S("gk_exp"), 2)
            V.scalar_tensor_tensor(eg[:], zg[:], 0.0, eg[:], ALU.min, ALU.subtract).then_inc(S("gk_log"), 1)
            v.wait_ge(S("gk_log"), 1)
            v.wait_ge(S("reset_set"), 2)
            V.tensor_tensor_scan(bg[:].rearrange(flat), attn_g[:].rearrange(flat), eg[:].rearrange(flat), 0.0, ALU.mult, ALU.add)\
                .then_inc(S("gk_sum"), 1)
            v.wait_ge(S("gk_sum"), 1)
            V.memset(attn_g[:], 0.0).then_inc(S("attn_zero"), 1)
            v.wait_ge(S("attn_zero"), 1)

            b_chunk = bg[:].rearrange("p h (t c) -> p (h t) c", c=P)
            V.tensor_tensor(eg[:].rearrange("p h (t c) -> p (h t) c", c=P), b_chunk[:, :, P - 1:P].broadcast_to([P, LH * TT, P]),
                            b_chunk, ALU.subtract).then_inc(S("kd_diff"), 1)
            v.wait_ge(S("lqk_done"), LIN_QK)
            v.wait_ge(S("kd_exp"), 2)
            V.tensor_tensor(kd_chan[:], eg[:], kg[:], ALU.mult).then_inc(S("kd_scaled"), 1)
            v.wait_ge(S("kd_scaled"), 1)

            def merge(item):
                mask = (ident[:] if item == 0 else masks[:, item - 1, :]).bitcast(u32).unsqueeze(1).broadcast_to([P, TT, P])
                v.wait_ge(S("lev_mm"), item + 1)
                for h in range(LH):
                    dst, src = attn_g[:, h, :].rearrange("p (t c) -> p t c", c=P), ps[:, 4 + h, :].rearrange("p (t c) -> p t c", c=P)
                    if item == 0:
                        mm = V.copy_predicated(dst, mask, src)
                    else:
                        mm = V.copy_predicated(halves(dst, item - 1, 1), halves(mask, item - 1, 1), halves(src, item - 1, 1))
                mm.then_inc(S("lev_merged"), 1)

            for l in range(LEVELS):
                n = 1 << l

                def blocks(x):
                    return x[:].rearrange("p h t -> p (h t)").rearrange("p (b a n) -> p b a n", a=2, n=n)
                b4, e4, z4 = blocks(bg), blocks(eg), blocks(zg)
                mid = b4[:, :, 0, n - 1:n].broadcast_to([P, LH * T // (2 * n), n])
                if l:
                    v.wait_ge(S("lev_z"), l)
                V.tensor_tensor(e4[:, :, 0, :], mid, b4[:, :, 0, :], ALU.subtract)
                V.tensor_tensor(e4[:, :, 1, :], b4[:, :, 1, :], mid, ALU.subtract).then_inc(S("lev_diff"), 1)
                merge(l)
                v.wait_ge(S("lqk_done"), LIN_QK)
                v.wait_ge(S("lev_exp"), l + 1)
                V.tensor_tensor(z4[:, :, 0, :], blocks(kg)[:, :, 0, :], e4[:, :, 0, :], ALU.mult)
                V.tensor_tensor(z4[:, :, 1, :], blocks(qg)[:, :, 1, :], e4[:, :, 1, :], ALU.mult).then_inc(S("lev_z"), 1)
            for j in range(LIN_GATE):
                v.wait_ge(S("lv_done"), LIN_V + j + 1)
                V.tensor_tensor(gg[:, :, j, :], gg[:, :, j, :], norm_w2[:].unsqueeze(1).broadcast_to([P, TT, DV]), ALU.mult)\
                    .then_inc(S("lgate_done"), 1)
            merge(LEVELS)
            v.wait_ge(S("qe_exp"), 1)
            V.tensor_tensor(zg[:], qg[:], eg[:], ALU.mult).then_inc(S("qe_done"), 1)
            v.wait_ge(S("qe_done"), 1)
            for tt in range(TT - 1):
                for h in range(LH):
                    n = tt * LH + h
                    v.wait_ge(S("lkv_mm"), (n | 1) + 1)
                    kv = ps[:, n // 2, (n % 2) * DV:(n % 2 + 1) * DV]
                    if tt == 0:
                        V.tensor_copy(states[:, 0, h, :], kv).then_inc(S("st_done"), 1)
                    else:
                        v.wait_ge(S("st_done"), n - LH + 1)
                        V.scalar_tensor_tensor(states[:, tt, h, :], states[:, tt - 1, h, :], glast_exp[:, h, tt:tt + 1], kv,
                                               ALU.mult, ALU.add).then_inc(S("st_done"), 1)
            for tt in range(TT):
                inv_root(stat[:, 4 + tt, 0:LH], DV, EPS, 6 * TT + (tt + 1) * LH)
                v.wait_ge(S("lgate_done"), LIN_GATE)
                for h in range(LH):
                    og = V.scalar_tensor_tensor(gg[:, tt, h, :], ps[:, O_BANK[tt] + h // 2, (h % 2) * DV:(h % 2 + 1) * DV],
                                                stat[:, 4 + tt, h:h + 1], gg[:, tt, h, :], ALU.mult, ALU.mult)
                og.then_inc(S("lo_gated"), 1)
            for tt in range(TT):
                parts_low(3, tt, O_BANK[tt])
            layer_norm(2, "ln2", 6 * TT + TT * LH)

        @block.tensor
        def _(pe):
            X = nc.tensor

            def turn(o, x, n=P):
                return X.transpose(o, x, ident[0:n, 0:n])

            pe.wait_ge(S("c_in"), 32)
            pe.wait_ge(S("rows_in"), 16 * 5)
            pe.wait_ge(S("ident_in"), 16)
            turn(ps[:, 6, 0:KD + LH], rows[0:KD + LH, 0, :], KD + LH)
            turn(ps[:, 7, 16:16 + 4 * FC], rows[0:4 * FC, 1, :], 4 * FC)
            turn(ps[:, 7, 16 + 4 * FC:16 + 8 * FC], rows[0:4 * FC, 2, :], 4 * FC)
            turn(ps[:, 7, 16 + 8 * FC:16 + 8 * FC + P], rows[:, 3, :]).then_inc(S("rows_turned"), 1)

            def mod(j, units=range(4)):
                if j >= 2:
                    pe.wait_ge(S("mods_done"), j - 1)
                for n in units:
                    u = 4 * j + n
                    o = ps[:, 2 * (j % 2) + n // 2, (n % 2) * UC:(n % 2 + 1) * UC]
                    X.matmul(o, ident[0:ADA, u:u + 1].broadcast_to([ADA, P]), ada_rows[0:ADA, :], start=True, stop=False)
                    if n % 2 and j < 5:
                        pe.wait_ge(S("partials"), KD * (2 * j + n // 2 + 1))
                        mm = X.matmul(o, ones[:, 0:1].broadcast_to([P, P]), partial[:, j % 2, n // 2, :], start=False, stop=True)
                    else:
                        pe.wait_ge(ada_full[n], 16 * (j + 1))
                        for k in range(KD):
                            mm = X.matmul(o, c_col[:, k:k + 1].broadcast_to([P, P]), ada[:, n, k, :], start=False, stop=(k == KD - 1))
                    mm.then_inc(S("ada_used"), 1)

            pe.wait_ge(S("c_silu"), 1)
            pe.wait_ge(S("prepared"), 1)
            mod(0)
            mod(1)
            mod(2)
            pe.wait_ge(S("pool_in"), 64)
            pe.wait_ge(S("cols_done"), 3)
            for cb in range(KD):
                if cb >= 4:
                    pe.wait_ge(S("pooled_done"), cb - 3)
                for tt in range(TT):
                    pe.wait_ge(S("u_ready"), tt + 1)
                    c0, nc_ = band_start(tt), band_cols(tt)
                    mm = X.matmul(ps[:, 4 + cb % 4, c0:c0 + nc_], u_pool[:, tt, cb * P:(cb + 1) * P],
                                  pool_band[:, cb // 2, tt, 0:nc_], start=(tt == 0), stop=(tt == TT - 1), skip_group_check=True)
                mm.then_inc(S("pool_mm"), 1)
            def mixed(tt):
                if tt >= 2:
                    pe.wait_ge(S("x1_done"), tt - 1)
                for g in range(POOL_GROUPS):
                    for k in range(2):
                        mm = X.matmul(ps[:, 4 + 2 * (tt % 2) + g // 2, (g % 2) * GDIM:(g % 2 + 1) * GDIM],
                                      pooled[:, 2 * g + k, tt * P:(tt + 1) * P], pool_w[:, g, k, :], start=(k == 0), stop=(k == 1))
                mm.then_inc(S("y_mm"), 1)

            mod(3)
            pe.wait_ge(S("pooled_done"), KD)
            pe.wait_ge(S("prepared"), 2)
            mixed(0)
            mixed(1)
            mod(4)
            mixed(2)
            mixed(3)
            mod(5, [0])

            def turn_tile(x, b):
                for k in range(KD):
                    mm = turn(ps[:, b + k // 4, (k % 4) * P:(k % 4 + 1) * P], x[:, k * P:(k + 1) * P])
                mm.then_inc(S("turned"), 1)

            pe.wait_ge(S("x1_done"), TT)
            for tt in range(TT):
                if tt >= 2:
                    pe.wait_ge(S("parts_lo"), tt - 1)
                pe.wait_ge(S("u2_ready"), tt + 1)
                turn_tile(u_ffn[:, tt, :], 4 + 2 * (tt % 2))
                if tt != 2:
                    mod(5, [min(tt + 1, 3)])

            def col_chunk(slot, sub, o):
                whk = wh[:, slot, :].rearrange("p (k n) -> p k n", n=UC)
                wlk = wl[:, slot, :].rearrange("p (k n) -> p k n", n=UC)
                c = slice(sub * P, (sub + 1) * P)
                for k in range(KD):
                    mm = mm3(o, whk[:, k, c], wlk[:, k, c], xth[:, k, :], xtl[:, k, :], k == 0, k == KD - 1)
                return mm

            pe.wait_ge(S("parts_lo"), 1 * TT)
            pe.wait_ge(S("mods_done"), 6)
            with pe.Fori(0, UP // 2) as i:
                for s in range(2):
                    pe.wait_ge(unit_split, i * 2 + s + 1)
                    for sub in range(2):
                        pe.wait_ge(S("conv_done"), i * 4 + 2 * s + sub + 1)
                        col_chunk(s, sub, ps[:, 2 * s + sub, :]).then_inc(S("up_half") if sub == 0 else w_used, 1)

            def down_unit(stage, u0, n, lh, ll, ready, banks_read=None):
                for u in range(n):
                    slot = (u0 + u) % 2
                    whk = wh[:, slot, :].rearrange("p (k n) -> p k n", n=D)
                    wlk = wl[:, slot, :].rearrange("p (k n) -> p k n", n=D)
                    pe.wait_ge(unit_split, u0 + u + 1)

                    def product(tt, half, kk):
                        k = 2 * u + kk
                        c = slice(half * 512, half * 512 + 512)
                        return mm3(ps[:, 2 * tt + half, :], lh(k, tt), ll(k, tt), whk[:, kk, c], wlk[:, kk, c],
                                   k == 0, k == 2 * n - 1)
                    if u == 0 and banks_read:
                        for kk in range(2):
                            ready(kk)
                            for tt in range(TT // 2, TT):
                                for half in range(2):
                                    product(tt, half, kk)
                        banks_read()
                        for kk in range(2):
                            for tt in range(TT // 2):
                                for half in range(2):
                                    mm = product(tt, half, kk)
                        mm.then_inc(w_used, 1)
                    elif u < n - 1:
                        for kk in range(2):
                            ready(2 * u + kk)
                            for tt in range(TT):
                                for half in range(2):
                                    mm = product(tt, half, kk)
                        mm.then_inc(w_used, 1)
                    else:
                        ready(2 * u + 1)
                        for tt in range(TT):
                            for half in range(2):
                                for kk in range(2):
                                    mm = product(tt, half, kk)
                            mm.then_inc(S("proj_mm"), 1)
                        pe.wait_ge(S("proj_mm"), (stage + 1) * TT)
                        pe.sem_inc(w_used, 1)

            down_unit(0, U_DOWN, DOWN, lambda k, tt: act_parts_h[:, k % 4, tt * P:(tt + 1) * P],
                      lambda k, tt: act_parts_l[:, k % 4, tt * P:(tt + 1) * P], 
                      lambda k: pe.wait_ge(S("act_split"), k + 1), lambda: pe.wait_ge(S("conv_done"), 4 + 2 * FC))
            for tt in range(TT):
                pe.wait_ge(S("x2_done"), tt + 1)
                turn_tile(xres[:, tt, :], 2 * tt)

            pe.wait_ge(S("parts_lo"), 2 * TT)
            def qkv_unit(n, s):
                pe.wait_ge(unit_split, n + U_GIN + 1)
                for sub in range(2):
                    pe.wait_ge(S("qkv_conv"), n * 2 + sub + 1)
                    col_chunk((U_GIN + s) % 2, sub, ps[:, 2 * s + sub, :]).then_inc(S("qkv_half") if sub == 0 else w_used, 1)

            def sums(n, s):
                pe.wait_ge(S("sq_done"), n + 1)
                for sub in range(2):
                    for tt in range(TT):
                        c = (n * 2 + sub) * TT + tt
                        o = ps[:, 6, c:c + 1] if isinstance(c, int) else ps[:, 6, ds(c, 1)]
                        mm = X.matmul(o, squares[:, s, sub, tt * P:(tt + 1) * P], ones[:, 0:1], start=True, stop=True)
                mm.then_inc(S("ss_mm"), 1)

            def turn_values(h):
                pe.wait_ge(S("v_silu"), h * 2 + 2)
                pe.wait_ge(S("val_done"), h + 1)
                for tt in range(TT):
                    for sub in range(2):
                        b, o = 4 + tt // 2, (tt % 2) * DV + sub * P
                        mm = turn(ps[:, b, o:o + P], conv_v[:, sub, tt * P:(tt + 1) * P])
                mm.then_inc(S("v_turned"), 1)

            pe.sem_inc(S("ss_mm"), 2)
            pe.sem_inc(S("v_turned"), 1)
            pe.sem_inc(S("val_done"), 1)
            qkv_unit(0, 0)
            with pe.Fori(0, GIN_QK // 2 - 1) as i:
                for s in range(2):
                    qkv_unit(i * 2 + 1 + s, 1 - s)
                    sums(i * 2 + s, s)
            qkv_unit(GIN_QK - 1, 1)
            sums(GIN_QK - 2, 0)
            pe.wait_ge(S("ba_split"), 1)
            for k in range(KD):
                mm = mm3(ps[0:2 * H, 7, :], ba_h[:, k, :], ba_l[:, k, :], xth[:, k, :], xtl[:, k, :], k == 0, k == KD - 1)
            mm.then_inc(S("ba_mm"), 1)
            qkv_unit(GIN_QK, 0)
            sums(GIN_QK - 1, 1)
            pe.wait_ge(S("ba_exp"), 1)
            for tt in range(TT):
                o = 2 * H * (TT + tt)
                mm = turn(ps[:, 6, o:o + 2 * H], ba_cols[0:2 * H, tt * P:(tt + 1) * P], 2 * H)
            mm.then_inc(S("ba_turned"), 1)
            with pe.Fori(0, GIN_V // 2 - 1) as i:
                for s in range(2):
                    qkv_unit(i * 2 + GIN_QK + 1 + s, 1 - s)
                    turn_values(i * 2 + s)
            pe.wait_ge(S("glog_done"), 1)
            pe.wait_ge(S("masks_in"), 48)
            pe.wait_ge(S("prepared"), 1)
            glog = scal[:, GLOG].rearrange("p t h -> p (t h)")
            X.matmul(ps[:, 7, 64:96], tri[:], glog, start=True, stop=True)
            X.matmul(ps[:, 7, 96:128], ones[:, 0:1].broadcast_to([P, P]), glog, start=True, stop=True).then_inc(S("gc_mm"), 1)
            qkv_unit(GIN_QK + GIN_V - 1, 1)
            turn_values(GIN_V - 2)

            def token_unit(slot, b, midway=None):
                whk = wh[:, slot, :].rearrange("p (k n) -> p k n", n=UC)
                wlk = wl[:, slot, :].rearrange("p (k n) -> p k n", n=UC)
                for tt in range(TT):
                    if midway and tt == TT // 2:
                        midway()
                    o = ps[:, b + tt // 2, (tt % 2) * UC:(tt % 2 + 1) * UC]
                    c = slice(tt * P, (tt + 1) * P)
                    for k in range(KD):
                        mm = mm3(o, xth[:, k, c], xtl[:, k, c], whk[:, k, :], wlk[:, k, :], k == 0, k == KD - 1)
                mm.then_inc(w_used, 1)

            u0 = U_GIN + GIN_QK + GIN_V
            for n in range(2):
                pe.wait_ge(unit_split, u0 + n + 1)
                pe.wait_ge(S("qkv_conv"), 4 + 2 * (GIN_QK + GIN_V) - 2 + 2 * n)
                token_unit((u0 + n) % 2, 2 * n)
                if n == 0:
                    turn_values(GIN_V - 1)
            with pe.Fori(1, GIN_GATE // 2) as i:
                for s in range(2):
                    pe.wait_ge(unit_split, i * 2 + u0 + s + 1)
                    pe.wait_ge(S("gate_silu"), i * 2 + s - 1)
                    token_unit((u0 + s) % 2, 2 * s)

            pe.sem_inc(S("vn_mm"), 1)
            pe.wait_ge(S("gate_silu"), GIN_GATE)
            with pe.Fori(0, TT) as i:
                tok = ds(i * P, P)

                def head(b, h):
                    return ps[:, b, (h % 4) * P:(h % 4 + 1) * P]

                def half(banks, h):
                    return ps[:, banks[h // 2], (h % 2) * DV:(h % 2 + 1) * DV]

                pe.wait_ge(S("staged"), i * 2 + 2)
                for g in range(2):
                    for h in range(4 * g, 4 * g + 4):
                        mm = X.matmul(head(2 * g, h), scal_now[:, GLOG, h:h + 1].broadcast_to([P, P]), tri[:], start=True, stop=True)
                    mm.then_inc(S("gcrow_mm"), 1)
                pe.wait_ge(S("ogt_lo"), i * 4 + 1)
                for g in range(2):
                    for h in range(4 * g, 4 * g + 4):
                        b, o = (1, 3, 4, 5)[h // 2], (h % 2) * 2 * P
                        mm = X.matmul(ps[:, b, o:o + 2 * P], k_now[:, h, :], qkt[:, :, h, tok], start=True, stop=True)
                    mm.then_inc(S("raw_mm"), 1)
                for h in range(H):
                    mm = turn(head(6 + h // 4, h), k_now[:, h, :])
                mm.then_inc(S("ktok_mm"), 1)
                for g in range(2):
                    pe.wait_ge(S("y0_done"), i * 2 + g + 1)
                    pe.wait_ge(S("attn_raw"), i * 2 + g + 1)
                    pe.wait_ge(S("eg_done"), i * 2 + g + 1)
                    for h in range(4 * g, 4 * g + 4):
                        mm = turn(head(2 * g, h), tri_inv[:, h, :])
                    mm.then_inc(S("x0_mm"), 1)
                for l in range(1, LEVELS):
                    for g in range(2):
                        pe.wait_ge(S("um_done"), i * 14 + 2 * l + g + 1)
                        if l == 1:
                            pe.wait_ge(S("x0_done"), i * 2 + g + 1)
                        else:
                            pe.wait_ge(S("xy_done"), i * 12 + 2 * (l - 2) + g + 1)
                        for h in range(4 * g, 4 * g + 4):
                            mm = X.matmul(head(2 * g, h), upper_m[:, h, :], tri_inv_t[:, h, :], start=True, stop=True)
                        mm.then_inc(S("p1_mm"), 1)
                    for g in range(2):
                        pe.wait_ge(S("p1_done"), i * 12 + 2 * (l - 1) + g + 1)
                        for h in range(4 * g, 4 * g + 4):
                            if l < LEVELS - 1:
                                X.matmul(head(2 * g + 1, h), tri_inv[:, h, :], prod[:, h, :], start=True, stop=True)
                            mm = X.matmul(head(4 + g, h), prod[:, h, :], tri_inv[:, h, :], start=True, stop=True)
                        mm.then_inc(S("xy_mm"), 1)
                for g in range(2):
                    pe.wait_ge(S("yfin_done"), i * 2 + g + 1)
                    pe.wait_ge(S("kin_done"), i * 2 + g + 1)
                    for h in range(4 * g, 4 * g + 4):
                        mm = X.matmul(head(2 * g, h), k_in[:, h, :], tri_inv[:, h, :], start=True, stop=True)
                    mm.then_inc(S("w_mm"), 1)
                for h in range(H):
                    o = half((1, 3, 4, 5), h)
                    if h % 4 == 0:
                        pe.wait_ge(S("w_done"), i * 2 + h // 4 + 1)
                    X.matmul(o, tri_inv[:, h, :], val[:, ds(i, 1), h, :].rearrange("p a n -> p (a n)"), start=True, stop=False)
                    X.matmul(o, part[:, h, :], state[:, h, :], start=False, stop=True).then_inc(S("vn_mm"), 1)
                for h in range(H):
                    if h % 4 == 0:
                        pe.wait_ge(S("kdec_done"), i * 2 + 2)
                    pe.wait_ge(S("vn_done"), i * H + (h | 1) + 1)
                    o = half((0, 2, 6, 7), h)
                    vn = val[:, ds(i, 1), h, :].rearrange("p a n -> p (a n)")
                    X.matmul(o, q_dec[:, h, :], state[:, h, :], start=True, stop=False)
                    X.matmul(o, attn[:, h, :], vn, start=False, stop=True).then_inc(S("o_mm"), 1)
                    X.matmul(half((1, 3, 4, 5), h), k_dec[:, h, :], vn, start=True, stop=True).then_inc(S("kv_mm"), 1)
                for b in range(4):
                    pe.wait_ge(S("s_done"), i * H + 2 * b + 2)
                    pe.wait_ge(S("og_done"), i * H + 2 * b + 2)
                    for k in range(4):
                        n = 4 * b + k
                        mm = turn(ps[:, (1, 3, 4, 5)[b], k * P:(k + 1) * P], gated_now[:, n // 2, (n % 2) * P:(n % 2 + 1) * P])
                    mm.then_inc(S("og_turned"), 1)

            pe.wait_ge(S("ogt_lo"), 4 * TT + 1)
            down_unit(1, U_GOUT, GOUT, lambda k, tt: ogt_h[:, tt, k, :], lambda k, tt: ogt_l[:, tt, k, :], lambda k: None)
            for tt in range(TT):
                pe.wait_ge(S("ln1_done"), tt + 1)
                turn_tile(xres[:, tt, :], 2 * tt)

            pe.wait_ge(S("parts_lo"), 3 * TT)
            pe.wait_ge(S("low_split"), 1)
            for k in range(KD):
                mm = mm3(ps[0:16, 0, :], low_h[:, k, :], low_l[:, k, :], xth[:, k, :], xtl[:, k, :], k == 0, k == KD - 1)
            mm.then_inc(S("low_mm"), 1)
            for j in range(LIN_QK):
                u, b = U_LIN + j, 2 * (j % 2)
                pe.wait_ge(unit_split, u + 1)
                if j == 0:
                    pe.wait_ge(S("gk_low_done"), 1)
                if j >= 2:
                    pe.wait_ge(S("lqk_done"), j - 1)
                col_chunk(u % 2, 0, ps[:, b, :])
                col_chunk(u % 2, 1, ps[:, b + 1, :]).then_inc(w_used, 1)
                if j == 0:
                    for h in range(LH):
                        X.matmul(ps[:, 4 + h, :], gk_up[0:16, h * DK:(h + 1) * DK], gk_low[0:16, :], start=True, stop=True)\
                            .then_inc(S("gk_mm"), 1)
            def turn_keys():
                pe.wait_ge(S("lev_merged"), 1)
                pe.wait_ge(S("kd_scaled"), 1)
                for h in range(LH):
                    for tt in range(TT):
                        mm = turn(ps[:, 4 + h, tt * P:(tt + 1) * P], kd_chan[:, h, tt * P:(tt + 1) * P])
                    mm.then_inc(S("kd_turned"), 1)

            for j in range(LIN_V + LIN_GATE):
                u, b = U_LIN + LIN_QK + j, 2 * (j % 2)
                pe.wait_ge(unit_split, u + 1)
                if j < 2:
                    pe.wait_ge(S("lqk_done"), LIN_QK - 1 + j)
                else:
                    pe.wait_ge(S("lv_done"), j - 1)
                token_unit(u % 2, b, turn_keys if j == 1 else None)
                if j == 1:
                    pe.wait_ge(S("kd_done"), LH)
                if j == 0:
                    pe.wait_ge(S("lqk_done"), LIN_QK)
                    pe.wait_ge(S("gk_z"), LH)
                else:
                    pe.wait_ge(S("lev_merged"), j)
                    pe.wait_ge(S("lev_z"), j)
                for h in range(LH):
                    for tt in range(TT):
                        c = slice(tt * P, (tt + 1) * P)
                        mm = X.matmul(ps[:, 4 + h, c], (kg if j == 0 else zg)[:, h, c], (qg if j == 0 else zg)[:, h, c],
                                      start=True, stop=True)
                mm.then_inc(S("lev_mm"), 1)
            for tt in range(TT - 1):
                if tt < 2:
                    pe.wait_ge(S("lv_done"), LIN_V + LIN_GATE - 1 + tt)
                else:
                    pe.wait_ge(S("lev_merged"), LEVELS + 1)
                for h in range(LH):
                    n = tt * LH + h
                    X.matmul(ps[:, n // 2, (n % 2) * DV:(n % 2 + 1) * DV], kd_tok[:, h, tt, :], vg[:, tt, h, :], start=True, stop=True)\
                        .then_inc(S("lkv_mm"), 1)
            for tt in range(TT):
                if tt >= 1:
                    pe.wait_ge(S("st_done"), tt * LH)
                for h in range(LH):
                    c = slice(tt * P, (tt + 1) * P)
                    o = ps[:, O_BANK[tt] + h // 2, (h % 2) * DV:(h % 2 + 1) * DV]
                    mm = X.matmul(o, attn_g[:, h, c], vg[:, tt, h, :], start=True, stop=(tt == 0))
                    if tt >= 1:
                        mm = X.matmul(o, zg[:, h, c], states[:, tt - 1, h, :], start=False, stop=True)
                    mm.then_inc(S("lo_mm"), 1)
            for tt in range(TT):
                pe.wait_ge(S("lo_gated"), tt + 1)
                turn_tile(gg[:, tt].rearrange("p h n -> p (h n)"), O_BANK[tt])
            pe.wait_ge(S("parts_lo"), 4 * TT)
            down_unit(2, U_LOUT, LOUT, lambda k, tt: xth[:, k, tt * P:(tt + 1) * P], lambda k, tt: xtl[:, k, tt * P:(tt + 1) * P],
                      lambda k: None)


def constants():
    import numpy as np
    s, c = np.arange(P)[:, None], np.arange(P)[None, :]
    parts = [s == c, s <= c]
    for l in range(LEVELS):
        n = 1 << l
        parts.append((s // (2 * n) == c // (2 * n)) & (s // n % 2 == 0) & (c // n % 2 == 1))
    consts = np.concatenate(parts, axis=1).astype(np.float32)
    band = np.zeros((P, POOL_GROUPS, TT, BAND), np.float32)
    for g, w in enumerate(POOL_WINDOWS):
        m = np.zeros((T, T), np.float32)
        for t in range(T):
            lo, hi = max(t - w // 2, 0), min(t + w // 2, T)
            m[lo:hi, t] = np.float32(1.0) / np.float32(hi - lo)
            m[t, t] -= np.float32(1.0)
        for tt in range(TT):
            band[:, g, tt, :band_cols(tt)] = m[tt * P:(tt + 1) * P, band_start(tt):band_start(tt) + band_cols(tt)]
    return {"consts": consts, "pool_band": band.reshape(P, -1)}


INPUTS = ["x", "c", "ada_w", "ada_b", "mix_pre_g", "mix_post_g", "ffn_pre_g", "ffn_post_g", "pool_w", "pool_scale",
          "ffn_w_up", "ffn_conv_w", "ffn_conv_b", "ffn_w_down",
          "gdn_w_in_2", "gdn_conv_w_2", "gdn_a_log_2", "gdn_dt_bias_2", "gdn_norm_w_2", "gdn_w_out_2",
          "gla_w_in_2", "gla_w_gk_up_2", "gla_b_gk_2", "gla_norm_w_2", "gla_w_out_2", "ln_g_2", "ln_b_2"]


def kernel(**inputs):
    import numpy as np
    import concourse.bacc as bacc
    from concourse.bass_utils import run_bass_kernel_spmd as run

    nc = bacc.Bacc("TRN2", target_bir_lowering=False, num_devices=1)
    arrays = {n: np.ascontiguousarray(inputs[n]) for n in INPUTS}
    arrays.update(constants())
    aps = {n: nc.dram_tensor("in_" + n, x.shape, mybir.dt.from_np(x.dtype), kind="ExternalInput").ap()
           for n, x in arrays.items()}
    out = nc.dram_tensor("out", (1, T, D), mybir.dt.float32, kind="ExternalOutput").ap()
    build(nc, aps, out)
    result = run(nc, [{"in_" + n: x for n, x in arrays.items()}], core_ids=[0])
    return result.results[0]["out"]
```
